# Optimizing a Trainium2 kernel written in Bass

```python
import math
import jax, jax.numpy as jnp
from jax import lax
import numpy as np
import jax
import jax.numpy as jnp

D_MODEL = 1024
BATCH = 1
SEQ = 512
DEPTH = 2

N_MIXERS = 2
N_HEADS = 16
HEAD_DIM = D_MODEL // N_HEADS
CONV_WIDTH = 3
BRANCHES = ((128, 1), (512, 4), (2048, 16))
NUM_BUCKETS = 32
MAX_DISTANCE = 2048
D_FF = ((8 * D_MODEL // 3 + 255) // 256) * 256
EPS = 1e-6
NEG_INF = -1e30


def rms_norm(x, g):
    xf = x.astype(jnp.float32)
    y = xf * lax.rsqrt(jnp.mean(xf * xf, axis=-1, keepdims=True) + EPS)
    return (y * g.astype(jnp.float32)).astype(x.dtype)

def t5_bucket(dist):
    exact = NUM_BUCKETS // 2
    df = jnp.maximum(dist, 1).astype(jnp.float32)
    large = exact + (jnp.log(df / exact) / math.log(MAX_DISTANCE / exact)
                     * (NUM_BUCKETS - exact)).astype(jnp.int32)
    large = jnp.minimum(large, NUM_BUCKETS - 1)
    return jnp.where(dist < exact, dist, large)

def short_conv_mixer(h, w_in, conv_k, w_out):
    b, c, u = jnp.split(h @ w_in, 3, axis=-1)
    y = lax.conv_general_dilated(
        c * u, conv_k[:, None, :].astype(u.dtype),
        window_strides=(1,), padding=[(CONV_WIDTH - 1, 0)],
        dimension_numbers=("NWC", "WIO", "NWC"),
        feature_group_count=D_MODEL)
    return (b * y) @ w_out

def dilated_branch(q, k, v, rel_bias, window, dilation):
    bsz, seq, nh, dh = q.shape
    blk = window // dilation
    L = seq // dilation
    nb = -(-L // blk)
    Lp = nb * blk

    def sub(t):
        t = t.reshape(bsz, L, dilation, nh, dh).transpose(0, 2, 1, 3, 4)
        t = jnp.pad(t, ((0, 0), (0, 0), (0, Lp - L), (0, 0), (0, 0)))
        return t.reshape(bsz, dilation, nb, blk, nh, dh)

    def with_prev(t):
        prev = jnp.pad(t, ((0, 0), (0, 0), (1, 0), (0, 0), (0, 0), (0, 0)))[:, :, :-1]
        return jnp.concatenate([prev, t], axis=3)

    qb = sub(q)
    kk = with_prev(sub(k))
    vv = with_prev(sub(v))

    s = jnp.einsum("brnqhd,brnkhd->brnhqk", qb, kk,
                   preferred_element_type=jnp.float32) * (HEAD_DIM ** -0.5)
    qi = jnp.arange(blk)[:, None]
    ki = jnp.arange(2 * blk)[None, :]
    rel = qi + blk - ki
    band = (rel >= 0) & (rel <= blk)
    valid_start = (jnp.arange(nb)[:, None, None] > 0) | (ki >= blk)[None]
    mask = band[None] & valid_start
    bias = rel_bias[t5_bucket(jnp.clip(rel, 0) * dilation)]
    s = s + bias.transpose(2, 0, 1).astype(jnp.float32)
    s = jnp.where(mask[:, None], s, NEG_INF)
    lse = jax.nn.logsumexp(s, axis=-1)
    p = jnp.exp(s - lse[..., None])
    o = jnp.einsum("brnhqk,brnkhd->brnqhd", p.astype(v.dtype), vv,
                   preferred_element_type=jnp.float32)

    o = o.reshape(bsz, dilation, Lp, nh, dh)[:, :, :L]
    o = o.transpose(0, 2, 1, 3, 4).reshape(bsz, seq, nh, dh)
    lse = lse.transpose(0, 1, 2, 4, 3).reshape(bsz, dilation, Lp, nh)[:, :, :L]
    lse = lse.transpose(0, 2, 1, 3).reshape(bsz, seq, nh)
    return o, lse

def dilated_attention_mixer(h, w_qkv, w_out, rel_bias):
    bsz, seq, _ = h.shape
    qkv = (h @ w_qkv).reshape(bsz, seq, 3, N_HEADS, HEAD_DIM)
    q, k, v = qkv[:, :, 0], qkv[:, :, 1], qkv[:, :, 2]
    outs, lses = [], []
    for window, dilation in BRANCHES:
        o, l = dilated_branch(q, k, v, rel_bias, window, dilation)
        outs.append(o)
        lses.append(l)
    alpha = jax.nn.softmax(jnp.stack(lses, axis=0), axis=0)
    o = jnp.sum(alpha[..., None] * jnp.stack(outs, axis=0), axis=0)
    return o.reshape(bsz, seq, D_MODEL).astype(h.dtype) @ w_out

def swiglu(h, w_gate, w_up, w_down):
    return (jax.nn.silu(h @ w_gate) * (h @ w_up)) @ w_down

def first_inputs(seed: int = 0) -> dict:
    key = jax.random.key(seed)
    ks = jax.random.split(key, 14)
    n_conv = (DEPTH + 1) // 2
    n_attn = DEPTH // 2
    f32 = jnp.float32
    nrm = lambda k, shape, scale: jax.random.normal(k, shape, f32) * scale
    return {
        "x": nrm(ks[0], (BATCH, SEQ, D_MODEL), 1.0),
        "mix_norm": 1.0 + nrm(ks[1], (DEPTH, D_MODEL), 0.05),
        "ffn_norm": 1.0 + nrm(ks[2], (DEPTH, D_MODEL), 0.05),
        "final_norm": 1.0 + nrm(ks[3], (D_MODEL,), 0.05),
        "conv_w_in": nrm(ks[4], (n_conv, D_MODEL, 3 * D_MODEL), D_MODEL ** -0.5),
        "conv_kernel": nrm(ks[5], (n_conv, CONV_WIDTH, D_MODEL), CONV_WIDTH ** -0.5),
        "conv_w_out": nrm(ks[6], (n_conv, D_MODEL, D_MODEL), D_MODEL ** -0.5),
        "attn_w_qkv": nrm(ks[7], (n_attn, D_MODEL, 3 * D_MODEL), D_MODEL ** -0.5),
        "attn_w_out": nrm(ks[8], (n_attn, D_MODEL, D_MODEL), D_MODEL ** -0.5),
        "rel_bias": nrm(ks[9], (NUM_BUCKETS, N_HEADS), 0.2),
        "ffn_w_gate": nrm(ks[10], (DEPTH, D_MODEL, D_FF), D_MODEL ** -0.5),
        "ffn_w_up": nrm(ks[11], (DEPTH, D_MODEL, D_FF), D_MODEL ** -0.5),
        "ffn_w_down": nrm(ks[12], (DEPTH, D_FF, D_MODEL), D_FF ** -0.5),
    }

def first_block(x, mix_norm, ffn_norm, final_norm, conv_w_in, conv_kernel, conv_w_out,
              attn_w_qkv, attn_w_out, rel_bias, ffn_w_gate, ffn_w_up, ffn_w_down):
    for i in range(DEPTH):
        h = rms_norm(x, mix_norm[i])
        j = i // N_MIXERS
        if i % N_MIXERS == 0:
            x = x + short_conv_mixer(h, conv_w_in[j], conv_kernel[j], conv_w_out[j])
        else:
            x = x + dilated_attention_mixer(h, attn_w_qkv[j], attn_w_out[j], rel_bias)
        h = rms_norm(x, ffn_norm[i])
        x = x + swiglu(h, ffn_w_gate[i], ffn_w_up[i], ffn_w_down[i])
    return rms_norm(x, final_norm)


N_MIXERS_2 = 4
EXPAND = 2
D_INNER = EXPAND * D_MODEL

SSD_HEAD_DIM = 64
SSD_HEADS = D_INNER // SSD_HEAD_DIM
SSD_GROUPS = 8
SSD_HPG = SSD_HEADS // SSD_GROUPS
SSD_STATE = 128
SSD_CONV = 5
SSD_CHUNK = 128
SSD_CONV_DIM = D_INNER + 2 * SSD_GROUPS * SSD_STATE
SSD_PROJ = D_INNER + SSD_CONV_DIM + 2 * SSD_HEADS

GLA_HEADS = 4
GLA_DK = D_MODEL // 2 // GLA_HEADS
GLA_DV = D_INNER // GLA_HEADS
GLA_RANK = 16
GLA_NORMALIZER = 16.0
GLA_CHUNK = 64
GLA_QK = GLA_HEADS * GLA_DK
GLA_PROJ = 2 * GLA_QK + 2 * D_INNER + 2 * GLA_RANK

HY_ORDER = 2
HY_SHORT = 3
HY_EMB = 33
HY_BANDS = (HY_EMB - 1) // 2
HY_FFN = 64
HY_INNER = 2
HY_FAST_PCT = 0.3
HY_SLOW_PCT = 1.5
HY_TARGET = 1e-2
HY_PROJ = (HY_ORDER + 2) * D_INNER
HY_FILT = 2 * HY_ORDER * D_INNER

ML_HEADS = 4
ML_DH = D_INNER // ML_HEADS
ML_DK = ML_DH // 2
ML_CONV = 5
ML_CHUNK = 64
ML_PROJ = 3 * D_INNER + 4 * ML_HEADS


def rmsnorm(x, g):
    xf = x.astype(jnp.float32)
    y = xf * lax.rsqrt(jnp.mean(xf * xf, axis=-1, keepdims=True) + EPS)
    return (y * g.astype(jnp.float32)).astype(x.dtype)

def dwconv(x, w, b):
    k = w.shape[0]
    y = lax.conv_general_dilated(x, w[:, None, :].astype(x.dtype), (1,), [((k - 1) // 2, (k - 1) // 2)],
                                 dimension_numbers=('NWC', 'WIO', 'NWC'), feature_group_count=x.shape[-1])
    return y + b.astype(x.dtype)

def rev(t):
    return jnp.flip(t, axis=1)

def to_chunks(t, q):
    b, l = t.shape[0], t.shape[1]
    return jnp.moveaxis(t.reshape((b, l // q, q) + t.shape[2:]), 1, 0)

def from_chunks(t):
    t = jnp.moveaxis(t, 0, 1)
    return t.reshape((t.shape[0], t.shape[1] * t.shape[2]) + t.shape[3:])

def ssd_scan(xh, dt, a, bm, cm):
    bsz, seq = xh.shape[:2]
    grp = (SSD_GROUPS, SSD_HPG)
    xs = to_chunks(xh.reshape((bsz, seq) + grp + (SSD_HEAD_DIM,)), SSD_CHUNK)
    dts = to_chunks(dt.reshape((bsz, seq) + grp), SSD_CHUNK)
    las = to_chunks((dt * a).reshape((bsz, seq) + grp), SSD_CHUNK)
    bs = to_chunks(bm, SSD_CHUNK)
    cs = to_chunks(cm, SSD_CHUNK)
    causal = jnp.tril(jnp.ones((SSD_CHUNK, SSD_CHUNK), bool))[None, :, :, None, None]

    def step(state, inp):
        xc, dtc, lac, bc, cc = inp
        cum = jnp.cumsum(lac, axis=1)
        decay = jnp.exp(jnp.where(causal, cum[:, :, None] - cum[:, None], -jnp.inf))
        xdt = xc * dtc[..., None]
        cb = jnp.einsum('blgn,bsgn->blsg', cc, bc)
        y = jnp.einsum('blsgr,bsgrp->blgrp', cb[..., None] * decay, xdt)
        y = y + jnp.einsum('blgn,bgrpn->blgrp', cc, state) * jnp.exp(cum)[..., None]
        tail = jnp.exp(cum[:, -1:] - cum)
        state = (state * jnp.exp(cum[:, -1])[..., None, None]
                 + jnp.einsum('bsgn,bsgrp->bgrpn', bc, xdt * tail[..., None]))
        return state, y

    state0 = jnp.zeros((bsz,) + grp + (SSD_HEAD_DIM, SSD_STATE), jnp.float32)
    _, ys = lax.scan(step, state0, (xs, dts, las, bs, cs))
    return from_chunks(ys).reshape(xh.shape)

def ssd_mixer(u, w_in, conv_w, conv_b, dt_bias, a_log, d_skip, gnorm, w_out):
    f32 = jnp.float32
    bsz, seq = u.shape[:2]
    z, xbc, dt = jnp.split(u @ w_in, [D_INNER, D_INNER + SSD_CONV_DIM], axis=-1)
    xbc = jax.nn.silu(dwconv(xbc, conv_w, conv_b)).astype(f32)
    xh, bm, cm = jnp.split(xbc, [D_INNER, D_INNER + SSD_GROUPS * SSD_STATE], axis=-1)
    xh = xh.reshape(bsz, seq, SSD_HEADS, SSD_HEAD_DIM)
    bm = bm.reshape(bsz, seq, SSD_GROUPS, SSD_STATE)
    cm = cm.reshape(bsz, seq, SSD_GROUPS, SSD_STATE)
    dt = jax.nn.softplus(dt.astype(f32).reshape(bsz, seq, 2, SSD_HEADS) + dt_bias.astype(f32))
    a = -jnp.exp(a_log.astype(f32))
    y = (ssd_scan(xh, dt[:, :, 0], a[0], bm, cm)
         + rev(ssd_scan(rev(xh), rev(dt[:, :, 1]), a[1], rev(bm), rev(cm)))
         + xh * d_skip.astype(f32)[:, None])
    y = y.reshape(bsz, seq, D_INNER) * jax.nn.silu(z.astype(f32))
    y = rmsnorm(y.reshape(bsz, seq, SSD_GROUPS, D_INNER // SSD_GROUPS), gnorm.reshape(SSD_GROUPS, -1))
    return y.reshape(bsz, seq, D_INNER).astype(u.dtype) @ w_out

def gla_scan(q, k, v, lg):
    bsz = q.shape[0]
    causal = jnp.tril(jnp.ones((GLA_CHUNK, GLA_CHUNK), bool))[None, None]

    def step(s, inp):
        qc, kc, vc, gc = inp
        cum = jnp.cumsum(gc, axis=1)
        qg = qc * jnp.exp(cum)
        kg = kc * jnp.exp(-cum)
        att = jnp.where(causal, jnp.einsum('blhk,bshk->bhls', qg, kg), 0.0)
        o = jnp.einsum('bhls,bshv->blhv', att, vc) + jnp.einsum('blhk,bhkv->blhv', qg, s)
        kd = kc * jnp.exp(cum[:, -1:] - cum)
        s = s * jnp.exp(cum[:, -1])[..., None] + jnp.einsum('bshk,bshv->bhkv', kd, vc)
        return s, o

    s0 = jnp.zeros((bsz, GLA_HEADS, GLA_DK, GLA_DV), jnp.float32)
    _, os_ = lax.scan(step, s0, tuple(to_chunks(t, GLA_CHUNK) for t in (q, k, v, lg)))
    return from_chunks(os_)

def gla_mixer(u, w_in, w_gate, b_gate, onorm, w_out):
    f32 = jnp.float32
    bsz, seq = u.shape[:2]
    q, k, v, z, gl = jnp.split(u @ w_in, [GLA_QK, 2 * GLA_QK, 2 * GLA_QK + D_INNER, 2 * GLA_QK + 2 * D_INNER], axis=-1)
    q = q.astype(f32).reshape(bsz, seq, GLA_HEADS, GLA_DK) * (GLA_DK ** -0.5)
    k = k.astype(f32).reshape(bsz, seq, GLA_HEADS, GLA_DK)
    v = v.astype(f32).reshape(bsz, seq, GLA_HEADS, GLA_DV)
    gl = gl.astype(f32).reshape(bsz, seq, 2, GLA_RANK)
    lg = jax.nn.log_sigmoid(jnp.einsum('bldr,drk->bldk', gl, w_gate.astype(f32)) + b_gate.astype(f32)) / GLA_NORMALIZER
    lg = lg.reshape(bsz, seq, 2, GLA_HEADS, GLA_DK)
    o = gla_scan(q, k, v, lg[:, :, 0]) + rev(gla_scan(rev(q), rev(k), rev(v), rev(lg[:, :, 1])))
    o = rmsnorm(o, onorm).reshape(bsz, seq, D_INNER) * jax.nn.silu(z.astype(f32))
    return o.astype(u.dtype) @ w_out

def hyena_filters(seq_len, w_in, b_in, w_hid, b_hid, freq, w_out):
    f32 = jnp.float32
    t = jnp.linspace(0.0, 1.0, seq_len, dtype=f32)[:, None]
    pos = jnp.arange(seq_len, dtype=f32)[:, None]
    bands = jnp.linspace(1e-4, HY_BANDS - 1, HY_BANDS, dtype=f32)[None]
    ang = (2.0 * math.pi / seq_len) * pos * bands
    feats = jnp.concatenate([t, jnp.cos(ang), -jnp.sin(ang)], axis=-1)
    freq = freq.astype(f32)
    h = jnp.sin(freq[0] * (feats @ w_in.astype(f32) + b_in.astype(f32)))
    for j in range(HY_INNER):
        h = jnp.sin(freq[j + 1] * (h @ w_hid[j].astype(f32) + b_hid[j].astype(f32)))
    h = (h @ w_out.astype(f32)).reshape(seq_len, 2, HY_ORDER, D_INNER)
    max_decay = math.log(HY_TARGET) / HY_FAST_PCT
    min_decay = math.log(HY_TARGET) / HY_SLOW_PCT
    deltas = jnp.abs(jnp.linspace(min_decay, max_decay, D_INNER, dtype=f32))
    return h * jnp.exp(-t[:, :, None, None] * deltas)

def long_conv(y, h_f, h_b):
    seq = y.shape[1]
    k = jnp.concatenate([h_f, jnp.zeros_like(h_f[:1]), jnp.flip(h_b[1:], axis=0)], axis=0)
    yf = jnp.fft.rfft(y, n=2 * seq, axis=1)
    kf = jnp.fft.rfft(k, axis=0)
    return jnp.fft.irfft(yf * kf[None], n=2 * seq, axis=1)[:, :seq]

def hyena_mixer(u, w_in, conv_w, conv_b, ffn_w_in, ffn_b_in, ffn_w_hid, ffn_b_hid, ffn_freq, ffn_w_out, d_bias, w_out):
    f32 = jnp.float32
    seq = u.shape[1]
    proj = u @ w_in
    sig = dwconv(proj[..., :3 * D_INNER], conv_w, conv_b).astype(f32)
    z = proj[..., 3 * D_INNER:]
    v, x1, x2 = jnp.split(sig, 3, axis=-1)
    filt = hyena_filters(seq, ffn_w_in, ffn_b_in, ffn_w_hid, ffn_b_hid, ffn_freq, ffn_w_out)
    d_bias = d_bias.astype(f32)
    y = v
    for o, gate in enumerate((x1, x2)):
        y = gate * (long_conv(y, filt[:, 0, o], filt[:, 1, o]) + y * d_bias[o])
    y = y * jax.nn.silu(z.astype(f32))
    return y.astype(u.dtype) @ w_out

def mlstm_scan(q, k, v, li, lf):
    bsz = q.shape[0]
    causal = jnp.tril(jnp.ones((ML_CHUNK, ML_CHUNK), bool))[None, :, :, None]

    def step(carry, inp):
        c, n, m = carry
        qc, kc, vc, ic, fc = inp
        b = jnp.cumsum(fc, axis=1)
        logd = jnp.where(causal, b[:, :, None] - b[:, None] + ic[:, None], -jnp.inf)
        inter = b + m[:, None]
        m_row = jnp.maximum(jnp.max(logd, axis=2), inter)
        s = jnp.einsum('blhk,bshk->blsh', qc, kc) * jnp.exp(logd - m_row[:, :, None])
        scale = jnp.exp(inter - m_row)
        num = jnp.einsum('blsh,bshv->blhv', s, vc) + jnp.einsum('blhk,bhkv->blhv', qc, c) * scale[..., None]
        den = jnp.sum(s, axis=2) + jnp.einsum('blhk,bhk->blh', qc, n) * scale
        hc = num / jnp.maximum(jnp.abs(den), jnp.exp(-m_row))[..., None]
        tot = b[:, -1]
        lw = tot[:, None] - b + ic
        m_new = jnp.maximum(tot + m, jnp.max(lw, axis=1))
        w = jnp.exp(lw - m_new[:, None])
        dec = jnp.exp(tot + m - m_new)
        c = c * dec[..., None, None] + jnp.einsum('bsh,bshk,bshv->bhkv', w, kc, vc)
        n = n * dec[..., None] + jnp.einsum('bsh,bshk->bhk', w, kc)
        return (c, n, m_new), hc

    carry0 = (jnp.zeros((bsz, ML_HEADS, ML_DK, ML_DH), jnp.float32),
              jnp.zeros((bsz, ML_HEADS, ML_DK), jnp.float32),
              jnp.full((bsz, ML_HEADS), -jnp.inf, jnp.float32))
    _, hs = lax.scan(step, carry0, tuple(to_chunks(t, ML_CHUNK) for t in (q, k, v, li, lf)))
    return from_chunks(hs)

def mlstm_mixer(u, w_in, conv_w, conv_b, w_q, w_k, w_v, gate_b, skip, onorm, w_out):
    f32 = jnp.float32
    bsz, seq = u.shape[:2]
    xm, z, og, gates = jnp.split(u @ w_in, [D_INNER, 2 * D_INNER, 3 * D_INNER], axis=-1)
    ch = jax.nn.silu(dwconv(xm, conv_w, conv_b)).astype(f32).reshape(bsz, seq, ML_HEADS, ML_DH)
    xmh = xm.astype(f32).reshape(bsz, seq, ML_HEADS, ML_DH)
    q = jnp.einsum('blhd,hdk->blhk', ch, w_q.astype(f32))
    k = jnp.einsum('blhd,hdk->blhk', ch, w_k.astype(f32)) * (ML_DK ** -0.5)
    v = jnp.einsum('blhd,hde->blhe', xmh, w_v.astype(f32))
    g = gates.astype(f32).reshape(bsz, seq, 2, 2, ML_HEADS) + gate_b.astype(f32)
    li = g[:, :, :, 0]
    lf = jax.nn.log_sigmoid(g[:, :, :, 1])
    h = (mlstm_scan(q, k, v, li[:, :, 0], lf[:, :, 0])
         + rev(mlstm_scan(rev(q), rev(k), rev(v), rev(li[:, :, 1]), rev(lf[:, :, 1]))))
    h = jax.nn.sigmoid(og.astype(f32)).reshape(bsz, seq, ML_HEADS, ML_DH) * h
    h = rmsnorm(h, onorm) + skip.astype(f32) * ch
    h = h.reshape(bsz, seq, D_INNER) * jax.nn.silu(z.astype(f32))
    return h.astype(u.dtype) @ w_out

def second_inputs(seed: int = 0) -> dict:
    key = jax.random.key(seed)
    keys = iter(jax.random.split(key, 64))
    f32 = jnp.float32

    def nrm(shape, scale):
        return scale * jax.random.normal(next(keys), shape, f32)

    def gain(shape):
        return 1.0 + nrm(shape, 0.02)

    na, nb, nh, nm = (len(range(t, DEPTH, N_MIXERS_2)) for t in range(N_MIXERS_2))
    w_in_s = D_MODEL ** -0.5
    w_out_s = D_INNER ** -0.5
    x = nrm((BATCH, SEQ, D_MODEL), 1.0)
    dt0 = jnp.exp(jax.random.uniform(next(keys), (na, 2, SSD_HEADS), f32, math.log(1e-3), math.log(1e-1)))
    ssd_dt_bias = dt0 + jnp.log(-jnp.expm1(-dt0))
    ssd_a_log = jnp.log(jax.random.uniform(next(keys), (na, 2, SSD_HEADS), f32, 1.0, 16.0))
    ml_gate_b = jnp.concatenate([nrm((nm, 2, 1, ML_HEADS), 0.1),
                                 jnp.linspace(3.0, 6.0, ML_HEADS, dtype=f32) + nrm((nm, 2, 1, ML_HEADS), 0.1)], axis=2)
    return {
        "x": x,
        "ssd_norm": gain((na, D_MODEL)),
        "ssd_w_in": nrm((na, D_MODEL, SSD_PROJ), w_in_s),
        "ssd_conv_w": nrm((na, SSD_CONV, SSD_CONV_DIM), SSD_CONV ** -0.5),
        "ssd_conv_b": nrm((na, SSD_CONV_DIM), 0.02),
        "ssd_dt_bias": ssd_dt_bias,
        "ssd_a_log": ssd_a_log,
        "ssd_d": gain((na, SSD_HEADS)),
        "ssd_gnorm": gain((na, D_INNER)),
        "ssd_w_out": nrm((na, D_INNER, D_MODEL), w_out_s),
        "gla_norm": gain((nb, D_MODEL)),
        "gla_w_in": nrm((nb, D_MODEL, GLA_PROJ), w_in_s),
        "gla_w_gate": nrm((nb, 2, GLA_RANK, GLA_QK), GLA_RANK ** -0.5),
        "gla_b_gate": nrm((nb, 2, GLA_QK), 0.02),
        "gla_onorm": gain((nb, GLA_DV)),
        "gla_w_out": nrm((nb, D_INNER, D_MODEL), w_out_s),
        "hy_norm": gain((nh, D_MODEL)),
        "hy_w_in": nrm((nh, D_MODEL, HY_PROJ), w_in_s),
        "hy_conv_w": nrm((nh, HY_SHORT, 3 * D_INNER), HY_SHORT ** -0.5),
        "hy_conv_b": nrm((nh, 3 * D_INNER), 0.02),
        "hy_ffn_w_in": nrm((nh, HY_EMB, HY_FFN), HY_EMB ** -0.5),
        "hy_ffn_b_in": nrm((nh, HY_FFN), 0.1),
        "hy_ffn_w_hid": nrm((nh, HY_INNER, HY_FFN, HY_FFN), HY_FFN ** -0.5),
        "hy_ffn_b_hid": nrm((nh, HY_INNER, HY_FFN), 0.1),
        "hy_ffn_freq": gain((nh, HY_INNER + 1, HY_FFN)),
        "hy_ffn_w_out": nrm((nh, HY_FFN, HY_FILT), 0.05 * HY_FFN ** -0.5),
        "hy_d": nrm((nh, HY_ORDER, D_INNER), 1.0),
        "hy_w_out": nrm((nh, D_INNER, D_MODEL), w_out_s),
        "ml_norm": gain((nm, D_MODEL)),
        "ml_w_in": nrm((nm, D_MODEL, ML_PROJ), w_in_s),
        "ml_conv_w": nrm((nm, ML_CONV, D_INNER), ML_CONV ** -0.5),
        "ml_conv_b": nrm((nm, D_INNER), 0.02),
        "ml_w_q": nrm((nm, ML_HEADS, ML_DH, ML_DK), ML_DH ** -0.5),
        "ml_w_k": nrm((nm, ML_HEADS, ML_DH, ML_DK), ML_DH ** -0.5),
        "ml_w_v": nrm((nm, ML_HEADS, ML_DH, ML_DH), ML_DH ** -0.5),
        "ml_gate_b": ml_gate_b,
        "ml_skip": gain((nm, ML_HEADS, ML_DH)),
        "ml_onorm": gain((nm, ML_DH)),
        "ml_w_out": nrm((nm, D_INNER, D_MODEL), w_out_s),
        "final_norm": gain((D_MODEL,)),
    }

def second_block(x,
              ssd_norm, ssd_w_in, ssd_conv_w, ssd_conv_b, ssd_dt_bias, ssd_a_log, ssd_d, ssd_gnorm, ssd_w_out,
              gla_norm, gla_w_in, gla_w_gate, gla_b_gate, gla_onorm, gla_w_out,
              hy_norm, hy_w_in, hy_conv_w, hy_conv_b, hy_ffn_w_in, hy_ffn_b_in, hy_ffn_w_hid, hy_ffn_b_hid,
              hy_ffn_freq, hy_ffn_w_out, hy_d, hy_w_out,
              ml_norm, ml_w_in, ml_conv_w, ml_conv_b, ml_w_q, ml_w_k, ml_w_v, ml_gate_b, ml_skip, ml_onorm, ml_w_out,
              final_norm):
    h = x
    for i in range(DEPTH):
        kind, j = i % N_MIXERS_2, i // N_MIXERS_2
        if kind == 0:
            h = h + ssd_mixer(rmsnorm(h, ssd_norm[j]), ssd_w_in[j], ssd_conv_w[j], ssd_conv_b[j], ssd_dt_bias[j],
                              ssd_a_log[j], ssd_d[j], ssd_gnorm[j], ssd_w_out[j])
        elif kind == 1:
            h = h + gla_mixer(rmsnorm(h, gla_norm[j]), gla_w_in[j], gla_w_gate[j], gla_b_gate[j], gla_onorm[j],
                              gla_w_out[j])
        elif kind == 2:
            h = h + hyena_mixer(rmsnorm(h, hy_norm[j]), hy_w_in[j], hy_conv_w[j], hy_conv_b[j], hy_ffn_w_in[j],
                                hy_ffn_b_in[j], hy_ffn_w_hid[j], hy_ffn_b_hid[j], hy_ffn_freq[j], hy_ffn_w_out[j],
                                hy_d[j], hy_w_out[j])
        else:
            h = h + mlstm_mixer(rmsnorm(h, ml_norm[j]), ml_w_in[j], ml_conv_w[j], ml_conv_b[j], ml_w_q[j], ml_w_k[j],
                                ml_w_v[j], ml_gate_b[j], ml_skip[j], ml_onorm[j], ml_w_out[j])
    return rmsnorm(h, final_norm)


def setup_inputs(seed=0):
    out = dict(first_inputs(seed))
    for name, value in second_inputs(seed + 1).items():
        if name != "x":
            out[name + "_2"] = value
    return out


def reference(
    x, mix_norm, ffn_norm, final_norm, conv_w_in, conv_kernel, conv_w_out, attn_w_qkv,
    attn_w_out, rel_bias, ffn_w_gate, ffn_w_up, ffn_w_down, ssd_norm_2, ssd_w_in_2,
    ssd_conv_w_2, ssd_conv_b_2, ssd_dt_bias_2, ssd_a_log_2, ssd_d_2, ssd_gnorm_2, ssd_w_out_2,
    gla_norm_2, gla_w_in_2, gla_w_gate_2, gla_b_gate_2, gla_onorm_2, gla_w_out_2, hy_norm_2,
    hy_w_in_2, hy_conv_w_2, hy_conv_b_2, hy_ffn_w_in_2, hy_ffn_b_in_2, hy_ffn_w_hid_2,
    hy_ffn_b_hid_2, hy_ffn_freq_2, hy_ffn_w_out_2, hy_d_2, hy_w_out_2, ml_norm_2, ml_w_in_2,
    ml_conv_w_2, ml_conv_b_2, ml_w_q_2, ml_w_k_2, ml_w_v_2, ml_gate_b_2, ml_skip_2, ml_onorm_2,
    ml_w_out_2, final_norm_2,
):
    x = first_block(
        x, mix_norm, ffn_norm, final_norm, conv_w_in, conv_kernel, conv_w_out, attn_w_qkv,
        attn_w_out, rel_bias, ffn_w_gate, ffn_w_up, ffn_w_down,
    )
    return second_block(
        x, ssd_norm_2, ssd_w_in_2, ssd_conv_w_2, ssd_conv_b_2, ssd_dt_bias_2, ssd_a_log_2,
        ssd_d_2, ssd_gnorm_2, ssd_w_out_2, gla_norm_2, gla_w_in_2, gla_w_gate_2, gla_b_gate_2,
        gla_onorm_2, gla_w_out_2, hy_norm_2, hy_w_in_2, hy_conv_w_2, hy_conv_b_2, hy_ffn_w_in_2,
        hy_ffn_b_in_2, hy_ffn_w_hid_2, hy_ffn_b_hid_2, hy_ffn_freq_2, hy_ffn_w_out_2, hy_d_2,
        hy_w_out_2, ml_norm_2, ml_w_in_2, ml_conv_w_2, ml_conv_b_2, ml_w_q_2, ml_w_k_2,
        ml_w_v_2, ml_gate_b_2, ml_skip_2, ml_onorm_2, ml_w_out_2, final_norm_2,
    )


_drawn_inputs = setup_inputs


def setup_inputs(seed=0):
    import zlib

    import numpy as np

    out = dict(_drawn_inputs(seed))
    spreads = {}
    factors = {'ssd_d_2': 6.162,
     'ssd_gnorm_2': 3.195,
     'gla_norm_2': 3.527,
     'gla_b_gate_2': 8.0,
     'gla_onorm_2': 18.215,
     'final_norm_2': 8.001}
    for name, (base, spread) in spreads.items():
        noise = np.random.default_rng([zlib.crc32(name.encode()), seed]).standard_normal(out[name].shape)
        drawn = base * np.exp(spread * noise) if base else spread * noise
        out[name] = jnp.asarray(drawn.astype(out[name].dtype))
    for name, factor in factors.items():
        out[name] = (out[name] * factor).astype(out[name].dtype)
    return out
```

```python
from contextlib import ExitStack, contextmanager

import concourse.bass as bass
import numpy as np
from concourse import mybir

F32 = mybir.dt.float32
F32R = mybir.dt.float32r
I32 = mybir.dt.int32
ALU = mybir.AluOpType
ACT = mybir.ActivationFunctionType
AX_X = mybir.AxisListType.X
ds = bass.ds

P = 128
SEQ = 512
NT = SEQ // P
DM = 1024
KT = DM // P
DFF = 2816
FT = DFF // P
HEADS = 16
DI = 2048
IT = DI // P
SSD_GROUPS = 8
HPG = 4
SSD_HEADS = 32
GLA_HEADS = 4
GC = 64
NGC = SEQ // GC
RANK = 16
EPS = 1e-6
NEG = -1e30
NBUCKETS = 32
START_AT_ONE = """cu_done c_ready a_done0 a_done1 sil_ready0 sil_ready1 pt_ready o_done pv
y_bank_free skip_ready sz_squared
sz_ready sy_turned gate_mm go_mm att_used kd_turned gu_mm gv_ready go_free att_ready
gs_ready kdt_ready gz_used gz_ready gy_turned""".split()
S_ORDER = (0, 2, 1, 3)
UNIT = 2048
HALF_FFN = FT // 2

VEC_ROWS = [("mix_norm", 16), ("ffn_norm", 16), ("final_norm", 8), ("conv_kernel", 24), ("ssd_norm_2", 8),
            ("ssd_gnorm_2", 16), ("gla_norm_2", 8), ("gla_b_gate_2", 8), ("gla_onorm_2", 4), ("final_norm_2", 8)]
VEC = {}
_at = 0
for _name, _rows in VEC_ROWS:
    VEC[_name] = _at
    _at += _rows
NVEC = _at
TAP = 128

INPUTS = ["x", "mix_norm", "ffn_norm", "final_norm", "conv_w_in", "conv_kernel", "conv_w_out", "attn_w_qkv", "attn_w_out",
          "rel_bias", "ffn_w_gate", "ffn_w_up", "ffn_w_down", "ssd_norm_2", "ssd_w_in_2", "ssd_conv_w_2", "ssd_conv_b_2",
          "ssd_dt_bias_2", "ssd_a_log_2", "ssd_d_2", "ssd_gnorm_2", "ssd_w_out_2", "gla_norm_2", "gla_w_in_2",
          "gla_w_gate_2", "gla_b_gate_2", "gla_onorm_2", "gla_w_out_2", "final_norm_2"]

U_CONV_CU, U_CONV_B, U_CONV_OUT = 0, 8, 12
U_FFN0, U_DOWN0 = 16, 38
U_QKV, U_ATTN_OUT = 54, 66
U_FFN1, U_DOWN1 = 70, 92
U_XBC, U_SZ, U_SSD_OUT = 108, 124, 132
U_GQK, U_GV, U_GZ, U_GLA_OUT = 140, 144, 152, 160
U_END = 168

STAGES = ["conv", "ffn0", "attn", "ffn1", "mid", "ssd", "gla", "end"]


def bucket_rows():
    d = 511 - np.arange(640)
    df = np.maximum(d, 1).astype(np.float32)
    exact = NBUCKETS // 2
    large = exact + (np.log(df / np.float32(exact)) / np.float32(np.log(2048 / exact)) * (NBUCKETS - exact)).astype(np.int32)
    bucket = np.where(d < exact, d, np.minimum(large, NBUCKETS - 1))
    rows = np.zeros((NBUCKETS + 1, 640), np.float32)
    for b in range(NBUCKETS):
        rows[b] = (bucket == b) & (d >= 0)
    times = (d <= 128).astype(int) + (d % 4 == 0) + (d % 16 == 0)
    rows[NBUCKETS] = np.where((d >= 0) & (times > 0), np.log(np.maximum(times, 1)), NEG)
    return rows


class Chain:

    def __init__(self, eng, sem):
        self.eng, self.sem, self.n, self.extra = eng, sem, 0, 0

    def __call__(self, ins):
        ins.then_inc(self.sem, 1)
        self.n += 1
        self.eng.wait_ge(self.sem, self.n + self.extra)

    def note(self, ins):
        ins.then_inc(self.sem, 1)
        self.n += 1

    @contextmanager
    def loop(self, count, per, start=0):
        n0, extra0 = self.n, self.extra
        with self.eng.Fori(start, start + count) as i:
            self.extra = extra0 + per * (i - start)
            yield i
            assert self.n - n0 == per, (self.n - n0, per)
        self.n, self.extra = n0 + per * count, extra0


def build(nc, A, out, stop=None):
    stages = STAGES[:STAGES.index(stop) + 1] if stop else STAGES
    on = lambda name: name in stages
    ends = {"conv": U_FFN0, "ffn0": U_QKV, "attn": U_FFN1, "ffn1": U_XBC, "mid": U_XBC, "ssd": U_GQK, "gla": U_END, "end": U_END}
    u_end = ends[stages[-1]]
    toeplitz = nc.dram_tensor("toeplitz", (HEADS, 640), F32, kind="Internal").ap()

    with ExitStack() as ctx:
        def sb(name, shape, dt=F32, c=ctx):
            return c.enter_context(nc.sbuf_tensor(name, shape, dt))

        sems = {}

        def S(name):
            if name not in sems:
                sems[name] = ctx.enter_context(nc.semaphore(name))
            return sems[name]

        bank = [ctx.enter_context(nc.psum_tensor(f"bank{i}", [P, 512], F32)) for i in range(8)]

        xT = sb("xT", [P, KT * SEQ])
        raw = [sb(f"raw{i}", [P, UNIT]) for i in range(2)]
        whi = [sb(f"whi{i}", [P, UNIT], F32R) for i in range(2)]
        wlo = [sb(f"wlo{i}", [P, UNIT], F32R) for i in range(2)]
        hHi = sb("hHi", [P, KT * SEQ], F32R)
        hLo = sb("hLo", [P, KT * SEQ], F32R)
        ident = sb("ident", [P, P])
        ones = sb("ones", [P, P])
        LE = sb("LE", [P, P])
        GE = sb("GE", [P, P])
        GT = sb("GT", [P, P])
        LT = sb("LT", [P, P])
        vecT = sb("vecT", [P, TAP + 192])
        rstd = sb("rstd", [P, SEQ])
        stat = sb("stat", [P, 64])
        t32 = [sb(f"t32_{i}", [P, SEQ]) for i in range(2)]

        @contextmanager
        def scope(spec):
            with ExitStack() as c:
                yield {n: sb(n, s, d, c) for n, s, d in spec}

        def area(spec):
            with scope(spec) as m:
                return m

        R8, V = [P, KT * SEQ], [P, SEQ]
        m_in = area([("xtok", R8, F32), ("vrows", [P, 3 * P], F32)])
        m_conv = area([("cu", [P, KT * 514], F32), ("c0", V, F32), ("c1", V, F32), ("cacc", [P, 2 * SEQ], F32),
                       ("yHi", R8, F32R), ("yLo", R8, F32R)])
        m_ffn = [area([(f"f{j}aHi", [P, FT * SEQ], F32R), (f"f{j}aLo", [P, FT * SEQ], F32R),
                       (f"f{j}sil", [P, 2 * SEQ], F32)]) for j in range(2)]
        m_att = area([("qk", [P, 2 * KT * SEQ], F32), ("vtok", R8, F32), ("otok", R8, F32), ("qF", V, F32), ("qS", V, F32), ("kS", V, F32),
                      ("prob0", [P, 1280], F32), ("prob1", [P, 1280], F32), ("pT", [P, 1280], F32), ("G0", V, F32), ("G1", V, F32),
                      ("rb", [NBUCKETS + 1, HEADS], F32), ("bkt", [NBUCKETS + 1, 640], F32),
                      ("toe", [HEADS, 640], F32), ("ast", [P, 32], F32)])
        with scope([("sY", [P, NT * DI], F32)]) as m_y:
            m_ssd = area([("wdtHi", [P, KT * 64], F32R), ("wdtLo", [P, KT * 64], F32R),
                          ("dtb", [P, 64], F32), ("alog", [P, 64], F32), ("dsk", [P, 32], F32),
                          ("dt", [P, 256], F32), ("dtA", [P, 256], F32), ("la", [P, 256], F32),
                          ("ecum", [P, 256], F32), ("etot", [P, 256], F32), ("wst", [P, 256], F32),
                          ("xpad", [P, 4 * 516], F32), ("xc", [P, 4 * SEQ], F32), ("xt", [P, NT * 256], F32),
                          ("bt", [P, SEQ], F32), ("CB", [P, 2 * SEQ], F32), ("Rm", [P, 2 * SEQ], F32),
                          ("MT", [P, 4 * SEQ], F32), ("xdt", [P, 4 * 256], F32), ("xw", [P, 2 * 256], F32),
                          ("stt", [P, 2 * NT * 256], F32), ("yt", [P, 2 * 256], F32), ("xd", [P, 256], F32)])
            m_ssd2 = area([("szs", [P, 2 * SEQ], F32), ("sHi", R8, F32R), ("sLo", R8, F32R)])
            m_ssd.update(m_y)
        with scope([("gO", [P, NT * DI], F32)]) as m_o:
            with scope([("gQK", [P, 8 * SEQ], F32), ("lg", [P, 2 * SEQ], F32),
                        ("wgf", [2 * RANK, 1024], F32), ("wgs", [2 * RANK, 2 * P], F32), ("m64", [P, SEQ], F32),
                        ("mF", [P, P], F32), ("mB", [P, P], F32),
                        ("qg", [P, 2 * SEQ], F32), ("kg", [P, 2 * SEQ], F32), ("kdt", [P, SEQ], F32),
                        ("gdec", [P, 2 * NGC], F32), ("attF", [P, P], F32), ("attB", [P, P], F32),
                        ("gst", [P, 8 * SEQ], F32), ("gsb", [P, 2 * SEQ], F32)]) as m_gla:
                m_gla.update(area([("gv", [P, NT * SEQ], F32)]))
                m_gl = area([("wglHi", [P, KT * 32], F32R), ("wglLo", [P, KT * 32], F32R), ("gl", [P, NT * 32], F32)])
            m_gla2 = area([("gzs", [P, 2 * SEQ], F32), ("gHi", R8, F32R), ("gLo", R8, F32R)])
            m_gla.update(m_o)
        m_end = area([("otk", R8, F32)])

        def tile(t, k, n=SEQ):
            return t[:, ds(k * n, n)]

        def col(name, k=0):
            return vecT[:, ds(VEC[name] + k, 1)]

        def tapcol(tap, k):
            return vecT[:, ds(TAP + 32 * tap + k, 1)]

        def v3(ap, a):
            return ap.rearrange("p (a b) -> p a b", a=a)

        def bc(ap, n):
            return ap.unsqueeze(2).broadcast_to([ap.shape[0], ap.shape[1], n])

        def rep(ap, n):
            return ap.unsqueeze(1).broadcast_to([ap.shape[0], n, ap.shape[1]])

        def heads(name, c, d, g):
            return m_ssd[name][:, ds(64 * c + 32 * d + HPG * g, HPG)]

        def h4(ap):
            return ap.rearrange("p (h e) -> p h e", h=HPG)

        def xw_buf(step, d):
            return t32[step][:, 256 * d:256 * d + 256] if step < 2 else m_ssd["xw"][:, 256 * d:256 * d + 256]

        def ssd_chunk(step, d):
            return step if d == 0 else 3 - step

        raw_full = [S("raw_full0"), S("raw_full1")]
        w_hi, w_lo = S("w_hi"), S("w_lo")
        mm = S("mm")
        res_done = S("res_done")
        h_ready = S("h_ready")
        R_IN, R_CONV, R_FFN0, R_ATT, R_FFN1, R_MID, R_SSD, R_GLA = range(8)
        last_r = {"conv": 1, "ffn0": 2, "attn": 3, "ffn1": 4, "mid": 5, "ssd": 6, "gla": 7, "end": 7}[stages[-1]]

        block = ctx.enter_context(nc.Block())

        @block.sync
        def _(sp):
            sp.dma_start(v3(m_in["xtok"][:, :], NT), A["x"][0].rearrange("(t p) c -> p t c", p=P)).then_inc(S("x_in"), 16)
            for name, rows in VEC_ROWS:
                flat = A[name]
                flat = flat.rearrange({1: "(r p) -> r p", 2: "a (r p) -> (a r) p", 3: "a b (r p) -> (a b r) p"}[len(flat.shape)], p=P)
                sp.dma_start(m_in["vrows"][VEC[name]:VEC[name] + rows, 0:P], flat).then_inc(S("vec_in"), 16)
            taps = A["ssd_conv_w_2"][0].rearrange("a (r p) -> (a r) p", p=P)
            sp.dma_start(m_in["vrows"][:, P:2 * P], taps[0:P]).then_inc(S("vec_in"), 16)
            sp.dma_start(m_in["vrows"][0:32, 2 * P:3 * P], taps[P:160]).then_inc(S("vec_in"), 16)
            sp.dma_start(m_in["vrows"][32:64, 2 * P:3 * P], A["ssd_conv_b_2"].rearrange("a (r p) -> (a r) p", p=P)).then_inc(S("vec_in"), 16)

            def load(n, s, src):
                if not isinstance(n, int) or n >= 2:
                    sp.wait_ge(w_lo, n - 1)
                if isinstance(src, tuple):
                    dst = v3(raw[s][:, :], KT)
                    pieces = [(dst[:, :, P * e:P * (e + 1)], src[e]) for e in range(2)]
                else:
                    kt, w = src.shape[1:]
                    dst = v3(raw[s][:, 0:kt * w], kt)
                    cut = (kt + 1) // 2
                    pieces = [(dst[:, 0:cut, :], src[:, 0:cut, :]), (dst[:, cut:kt, :], src[:, cut:kt, :])]
                for to, frm in pieces:
                    sp.dma_start(to, frm).then_inc(raw_full[s], 16)

            def cols(W, at, n=256):
                return W.rearrange("(k p) n -> p k n", p=P)[:, :, ds(at, n)]

            def pairs(u0, n_pairs, src):
                with sp.Fori(0, n_pairs) as i:
                    for s in range(2):
                        load(u0 + 2 * i + s, s, src(i, s))

            W = A["conv_w_in"][0]
            for s in range(2):
                load(s, s, cols(W, (1 + s) * DM))
            for name in START_AT_ONE:
                sp.sem_inc(S(name), 1)
            with sp.Fori(1, 4) as i:
                for s in range(2):
                    load(2 * i + s, s, cols(W, (1 + s) * DM + 256 * i))
            pairs(U_CONV_B, 2, lambda i, s: cols(W, 512 * i + 256 * s))
            pairs(U_CONV_OUT, 2, lambda i, s: cols(A["conv_w_out"][0], 512 * i + 256 * s))

            def ffn(j, u_up, u_down):
                pairs(u_up, FT // 2, lambda i, s: cols(A[("ffn_w_gate", "ffn_w_up")[s]][j], 256 * i))
                down = A["ffn_w_down"][j]
                pairs(u_down, KT, lambda i, s: cols(down[HALF_FFN * P * s:HALF_FFN * P * (s + 1)], P * i, P))

            if on("ffn0"):
                ffn(0, U_FFN0, U_DOWN0)
            if on("attn"):
                pairs(U_QKV, 6, lambda i, s: cols(A["attn_w_qkv"][0], 512 * i + 256 * s))
                pairs(U_ATTN_OUT, 1, lambda i, s: cols(A["attn_w_out"][0], 512 * i + 256 * s))
                sp.wait_ge(S("toe_ready"), 1)
                sp.dma_start(toeplitz, m_att["toe"][:, :]).then_inc(S("toe_out"), 16)
                sp.wait_ge(S("toe_out"), 16)

                def bias_tile(pr, hh):
                    src = bass.AP(tensor=toeplitz.tensor, offset=640 * (2 * pr + hh), ap=[[1, P], [1, SEQ]])
                    sp.dma_start(m_att[f"G{hh}"][:, :], src).then_inc(S(f"g_in{hh}"), 16)

                for hh in range(2):
                    bias_tile(0, hh)
                with sp.Fori(1, HEADS // 2) as pr:
                    for hh in range(2):
                        sp.wait_ge(S("scored"), 4 * (2 * pr + hh - 1))
                        bias_tile(pr, hh)
                pairs(U_ATTN_OUT + 2, 1, lambda i, s: cols(A["attn_w_out"][0], 512 * (i + 1) + 256 * s))
            if on("ffn1"):
                ffn(1, U_FFN1, U_DOWN1)
            if on("ssd"):
                W = A["ssd_w_in_2"][0]
                pairs(U_XBC, 8, lambda i, s: tuple(cols(W, 2 * DI + DM * e + P * i, P) for e in range(2)) if s else cols(W, DI + 256 * i))
                pairs(U_SZ, 4, lambda i, s: cols(W, 512 * i + 256 * s))
                pairs(U_SSD_OUT, 4, lambda i, s: cols(A["ssd_w_out_2"][0], 256 * i + P * s, P))
            if on("gla"):
                W = A["gla_w_in_2"][0]
                pairs(U_GQK, 2, lambda i, s: tuple(cols(W, 512 * e + 256 * i + P * s, P) for e in range(2)))
                pairs(U_GV, 4, lambda i, s: cols(W, 1024 + 512 * i + 256 * s))
                pairs(U_GZ, 4, lambda i, s: cols(W, 1024 + DI + 512 * i + 256 * s))
                pairs(U_GLA_OUT, 4, lambda i, s: cols(A["gla_w_out_2"][0], 256 * i + P * s, P))
            for t in range(NT):
                sp.wait_ge(S("out_ready"), 8 * (t + 1))
                sp.dma_start(out[0, P * t:P * (t + 1), :], m_end["otk"][:, DM * t:DM * (t + 1)]).then_inc(S("out_done"), 16)
            sp.wait_ge(S("out_done"), 16 * NT)

        @block.gpsimd
        def _(pool):
            n = 0
            cst = S("cst")

            def step(ins):
                nonlocal n
                ins.then_inc(cst, 1)
                n += 1

            step(pool.memset(ident[:, :], 0.0))
            for m in (ones, LE, GE, GT, LT):
                step(pool.memset(m[:, :], 1.0))
            pool.wait_ge(cst, n)
            step(pool.affine_select(out=ident[:, :], in_=ident[:, :], compare_op=ALU.not_equal, fill=1.0, base=0,
                                    pattern=[[1, P]], channel_multiplier=-1))
            for m, op, sign in ((LE, ALU.is_ge, 1), (GE, ALU.is_ge, -1), (GT, ALU.is_gt, -1), (LT, ALU.is_gt, 1)):
                step(pool.affine_select(out=m[:, :], in_=m[:, :], compare_op=op, fill=0.0, base=0,
                                        pattern=[[sign, P]], channel_multiplier=-sign))
            assert n == 11

            def low(k, s):
                pool.wait_ge(w_hi, k)
                pool.tensor_tensor(wlo[s][:, :], raw[s][:, :], whi[s][:, :].bitcast(F32), ALU.subtract).then_inc(w_lo, 1)

            def lows(u0, u1):
                with pool.Fori(u0 // 2, u1 // 2) as i:
                    for s in range(2):
                        low(2 * i + s + 1, s)

            def ssd_group(g, split):
                m = m_ssd
                pool.wait_ge(S("xt_ready"), 3 * g + 2)
                for step in range(3):
                    for d in range(2):
                        c = ssd_chunk(step, d)
                        pool.tensor_tensor(h4(xw_buf(step, d)), h4(m["xt"][:, 256 * c:256 * c + 256]), bc(heads("wst", c, d, g), 64),
                                           ALU.mult).then_inc(S("xw_ready"), 1)
                for c in range(NT):
                    for d, mask in enumerate((LE, GE)):
                        if c:
                            pool.wait_ge(S("seg"), 8 * g + 2 * (c - 1) + d + 1)
                        pool.tensor_tensor(v3(m["Rm"][:, SEQ * d:SEQ * (d + 1)], HPG), bc(heads("la", c, d, g), P), rep(mask[:, :], HPG),
                                           ALU.mult).then_inc(S("rm_ready"), 1)
                    if c >= 2:
                        pool.wait_ge(S("y_mm"), 4 * g + c - 1)
                    for d in range(2):
                        at = 512 * (c % 2) + 256 * d
                        pool.tensor_tensor(h4(m["xdt"][:, at:at + 256]), h4(m["xt"][:, 256 * c:256 * c + 256]), bc(heads("dt", c, d, g), 64),
                                           ALU.mult).then_inc(S("xdt_ready"), 1)
                    if c == 2 and split:
                        low(U_XBC + 2 * g + 4 + 1, 0)
                if split == 2:
                    low(U_XBC + 2 * g + 5 + 1, 1)

            if on("ssd"):
                lows(0, U_XBC + 4)
                pool.wait_ge(S("la_ready"), 1)
                pool.wait_ge(S("wst_ready"), 1)
                with pool.Fori(0, SSD_GROUPS - 2) as g:
                    ssd_group(g, 2)
                ssd_group(SSD_GROUPS - 2, 1)
                ssd_group(SSD_GROUPS - 1, 0)
                low(U_SZ + 1 + 1, 1)
                lows(U_SZ + 2, u_end)
            else:
                lows(0, u_end)

        @block.scalar
        def _(act):
            chain = Chain(act, S("act_chain"))

            def high(n, s, k=None):
                act.wait_ge(raw_full[s], 32 * (n // 2 + 1 if k is None else k))
                if not isinstance(n, int) or n >= 2:
                    act.wait_ge(mm, 2 * (n - 1))
                act.activation(whi[s][:, :], raw[s][:, :], ACT.Copy).then_inc(w_hi, 1)

            def ahead(u0, i, s, per=2):
                if isinstance(i, int) and u0 + per * i + s + 1 >= u_end:
                    return
                high(u0 + per * i + s + 1, (s + 1) % 2, u0 // 2 + (per // 2) * i + (s + 1) // 2 + 1)

            def loop(u0, count, per=2, steps=0):
                if u0 + per * count < u_end:
                    with chain.loop(count, steps) as i:
                        yield i
                else:
                    if count > 1:
                        with chain.loop(count - 1, steps) as i:
                            yield i
                    yield count - 1

            def copy(dst, src, sem, scale=1.0):
                act.activation(dst, src, ACT.Copy, scale=scale).then_inc(sem, 1)

            def norm(j):
                for k in range(KT):
                    act.wait_ge(res_done, 8 * j + k + 1)
                    if 8 * j + k >= 2:
                        act.wait_ge(S("sq_used"), 8 * j + k - 1)
                    act.activation(t32[k % 2][:, :], tile(xT, k), ACT.Square).then_inc(S("sq_ready"), 1)
                act.wait_ge(S("mean_ready"), j + 1)
                act.activation(rstd[:, :], rstd[:, :], ACT.Sqrt).then_inc(S("root_ready"), 1)

            high(0, 0)
            act.wait_ge(S("vec_turned"), 3)
            copy(vecT[:, 0:NVEC], bank[4][:, 0:NVEC], S("vec_ready"))
            copy(vecT[:, TAP:TAP + 192], bank[4][:, TAP:TAP + 192], S("vec_ready"))

            norm(0)
            for i in loop(0, 4):
                for s in range(2):
                    ahead(0, i, s)
                    if s == 0:
                        for b in range(2):
                            act.wait_ge(mm, 4 * i + b + 1)
                            act.wait_ge(S("cu_done"), 2 * i + 1)
                            copy(m_conv[f"c{b}"][:, :], bank[b][:, :], S("c_ready"))
            for i in loop(U_CONV_B, 2):
                for s in range(2):
                    ahead(U_CONV_B, i, s)
            for i in loop(U_CONV_OUT, 2):
                for s in range(2):
                    ahead(U_CONV_OUT, i, s)

            def ffn(j, u_up, u_down):
                norm(2 * j + 1)
                for i in loop(u_up, FT // 2):
                    for s in range(2):
                        ahead(u_up, i, s)
                        if s == 0:
                            for b in range(2):
                                act.wait_ge(mm, 2 * u_up + 4 * i + b + 1)
                                act.wait_ge(S(f"a_done{j}"), 2 * i + 1)
                                act.activation(tile(m_ffn[j][f"f{j}sil"], b), bank[b][:, :], ACT.Silu).then_inc(S(f"sil_ready{j}"), 1)
                for i in loop(u_down, KT):
                    for s in range(2):
                        ahead(u_down, i, s)

            if on("ffn0"):
                ffn(0, U_FFN0, U_DOWN0)

            if on("attn"):
                act.wait_ge(res_done, 8 * (R_FFN0 + 1))
                act.dma_start(m_att["rb"][0:NBUCKETS, :], A["rel_bias"]).then_inc(S("bias_in"), 16)
                act.dma_start(m_att["bkt"][:, :], A["bucket_rows"]).then_inc(S("bias_in"), 16)
                act.wait_ge(S("toe_mm"), 2)
                copy(m_att["toe"][:, 0:SEQ], bank[5][0:HEADS, :], S("act_toe"))
                act.activation(m_att["toe"][:, SEQ:640], bank[6][0:HEADS, 0:P], ACT.Copy).then_inc(S("toe_half"), 1)
                act.wait_ge(S("act_toe"), 1)
                act.wait_ge(S("toe_half"), 1)
                act.sem_inc(S("toe_ready"), 1)
                norm(2)
                qk = m_att["qk"]
                act.sem_inc(S("qkv_free"), 4)
                for i in loop(U_QKV, 4):
                    for s in range(2):
                        ahead(U_QKV, i, s)
                        for b in range(2):
                            act.wait_ge(mm, 2 * U_QKV + 4 * i + 2 * s + b + 1)
                            copy(tile(qk, 4 * i + 2 * s + b), bank[2 * s + b][:, :], S("qkv_free"))
                vt = v3(m_att["vtok"][:, :], NT)
                for i in loop(U_QKV + 8, 2):
                    for s in range(2):
                        ahead(U_QKV + 8, i, s)
                        for hf in range(2):
                            act.wait_ge(mm, 2 * (U_QKV + 8) + 4 * i + 2 * s + hf + 1)
                            copy(vt[:, 2 * hf:2 * hf + 2, ds(512 * i + 256 * s, 256)], v3(bank[2 * s + hf][:, :], 2), S("qkv_free"))
                ast = m_att["ast"]

                def stage_q(pr):
                    act.wait_ge(S("scores"), 8 * pr)
                    copy(m_att["qF"][:, :], tile(qk, pr), S("qf_ready"), scale=64 ** -0.5)
                    copy(m_att["kS"][:, :], tile(qk, KT + pr), S("qs_ready"))
                    act.wait_ge(S("qf_ready"), pr + 1)
                    copy(v3(m_att["qS"][:, :], NT), v3(m_att["qF"][:, :], NT)[:, :, ::-1], S("qs_ready"))

                def softmax(pr, hh):
                    hd = 2 * pr + hh
                    prob, pT = m_att[f"prob{hh}"], m_att["pT"]
                    for n, i in enumerate(S_ORDER):
                        act.wait_ge(S("scored"), 4 * hd + n + 1)
                        reg = slice(64 * i * (i + 1), 64 * (i + 1) * (i + 2))
                        act.activation(prob[:, reg], prob[:, reg], ACT.Exp, bias=ast[:, 16 * hh + 4 + i:16 * hh + 5 + i],
                                       accum_out=ast[:, 16 * hh + 8 + i:16 * hh + 9 + i]).then_inc(S("prob_ready"), 1)
                    act.wait_ge(S("pv"), hd + 1)
                    for j in range(NT):
                        act.wait_ge(S("prob_turned"), 4 * hd + j + 1)
                        w = P * (NT - j)
                        at = [0, 512, 896, 1152][j]
                        copy(pT[:, at:at + w], bank[j][:, 0:w], S("pt_ready"))

                act.wait_ge(S("qkv_free"), 4 + 16 + 8)
                stage_q(0)
                with act.Fori(0, HEADS // 2 - 1) as pr:
                    softmax(pr, 0)
                    stage_q(pr + 1)
                    softmax(pr, 1)
                softmax(HEADS // 2 - 1, 0)
                softmax(HEADS // 2 - 1, 1)
                for i in loop(U_ATTN_OUT, 2):
                    for s in range(2):
                        ahead(U_ATTN_OUT, i, s)

            if on("ffn1"):
                ffn(1, U_FFN1, U_DOWN1)
            if on("mid"):
                norm(4)

            if on("ssd"):
                m = m_ssd
                act.wait_ge(S("mid_done"), 8)
                act.dma_start(v3(m_ssd["Rm"][:, 0:SEQ], KT), A["ssd_w_in_2"][0, :, DI + 4096:DI + 4096 + 64].rearrange("(k p) n -> p k n", p=P)).then_inc(S("ssd_in"), 16)
                for name, src in (("dtb", "ssd_dt_bias_2"), ("alog", "ssd_a_log_2")):
                    row = A[src].rearrange("a d h -> a (d h)")
                    act.dma_start(m_ssd[name][:, :], row.broadcast_to([P, 64])).then_inc(S("ssd_in"), 16)
                act.dma_start(m_ssd["dsk"][:, :], A["ssd_d_2"].broadcast_to([P, 32])).then_inc(S("ssd_in"), 16)
                act.wait_ge(S("ssd_in"), 64)
                act.activation(m["alog"][:, :], m["alog"][:, :], ACT.Exp).then_inc(S("a_exp"), 1)
                norm(5)
                act.wait_ge(S("dt_pre"), 1)
                chain(act.activation(m["dtA"][:, :], m["dt"][:, :], ACT.Abs))
                chain(act.activation(m["dtA"][:, :], m["dtA"][:, :], ACT.Exp, scale=-1.0))
                act.activation(m["dtA"][:, :], m["dtA"][:, :], ACT.Ln, bias=1.0).then_inc(S("dt_log"), 1)
                act.wait_ge(S("decays"), 1)
                for b, name in ((5, "ecum"), (6, "wst"), (7, "etot")):
                    act.activation(m[name][:, :], bank[b][:, 0:256], ACT.Exp).then_inc(S("decay_exp"), 1)

                def to_xpad(g, q):
                    act.wait_ge(mm, 2 * U_XBC + 4 * g + q + 1)
                    copy(m["xpad"][:, 516 * q + 2:516 * q + 514], bank[q][:, :], S("xpad_ready"))

                def silus(g):
                    for q in range(4):
                        ct = 2 * g + q if q < 2 else (16 if q == 2 else 24) + g
                        act.wait_ge(S("tap_done"), 4 * g + q + 1)
                        act.activation(tile(m["xc"], q), tile(m["xc"], q), ACT.Silu, bias=tapcol(5, ct)).then_inc(S("xc_ready"), 1)

                def group(g, more, split):
                    act.wait_ge(S("skip_ready"), 4 * g + 1)
                    for b in range(3):
                        act.wait_ge(S("x_turned"), 3 * g + b + 1)
                        dst = m["bt"][:, :] if b == 2 else m["xt"][:, 512 * b:512 * b + 512]
                        copy(dst, bank[4 + b][:, :], S("xt_ready"))
                    if more:
                        to_xpad(g + 1, 0)
                    for c in range(NT):
                        for d in range(2):
                            act.wait_ge(S("seg"), 8 * g + 2 * c + d + 1)
                            act.activation(tile(m["MT"], 2 * (c % 2) + d), bank[4 + d][:, :], ACT.Exp).then_inc(S("ex_ready"), 1)
                        if more and c < 3:
                            to_xpad(g + 1, c + 1)
                        if split and c == 1:
                            high(U_XBC + 2 * g + 4, 0, U_XBC // 2 + g + 3)
                    if more:
                        silus(g + 1)
                    if split == 2:
                        high(U_XBC + 2 * g + 5, 1, U_XBC // 2 + g + 3)

                high(U_XBC + 1, 1)
                for q in range(4):
                    to_xpad(0, q)
                    if q % 2:
                        high(U_XBC + 2 + q // 2, q // 2)
                silus(0)
                with act.Fori(0, SSD_GROUPS - 2) as g:
                    group(g, True, 2)
                group(SSD_GROUPS - 2, True, 1)
                group(SSD_GROUPS - 1, False, 0)
                for i in loop(U_SZ, 4):
                    for s in range(2):
                        ahead(U_SZ, i, s)
                        for hf in range(2):
                            act.wait_ge(mm, 2 * U_SZ + 4 * i + 2 * s + hf + 1)
                            zs = tile(m_ssd2["szs"], hf)
                            act.wait_ge(S("sz_squared"), 8 * i + 4 * s + 1)
                            act.activation(zs, bank[2 * s + hf][:, :], ACT.Silu).then_inc(S("sz_ready"), 1)
                            act.wait_ge(S("sz_used"), 4 * i + 2 * s + hf + 1)
                            for e in range(2):
                                act.activation(zs[:, 256 * e:256 * e + 256],
                                               v3(m_ssd["sY"][:, :], NT)[:, 2 * hf + e, ds(512 * i + 256 * s, 256)], ACT.Square,
                                               accum_out=stat[:, ds(8 * (2 * hf + e) + 2 * i + s, 1)]).then_inc(S("sz_squared"), 1)
                act.wait_ge(S("ssq_mean"), 1)
                act.activation(stat[:, 0:32], stat[:, 0:32], ACT.Sqrt).then_inc(S("ssq_root"), 1)
                for i in loop(U_SSD_OUT, 4):
                    for s in range(2):
                        ahead(U_SSD_OUT, i, s)

            if on("gla"):
                m = m_gla
                act.wait_ge(res_done, 8 * (R_SSD + 1))
                act.dma_start(v3(m_gla["kg"][:, 0:256], KT), A["gla_w_in_2"][0, :, 1024 + 2 * DI:1024 + 2 * DI + 32].rearrange("(k p) n -> p k n", p=P)).then_inc(S("gla_in"), 16)
                act.wait_ge(S("wgf_zero"), 1)
                for d in range(2):
                    act.dma_start(m_gla["wgf"][RANK * d:RANK * (d + 1), 512 * d:512 * (d + 1)],
                                 A["gla_w_gate_2"][0, d]).then_inc(S("gla_in"), 16)
                norm(6)
                act.wait_ge(S("gl_mm"), 1)
                copy(m_gl["gl"][:, :], bank[4][:, 0:128], S("gl_ready"))
                act.wait_ge(S("gl_turned"), 1)
                act.activation(rstd[0:32, :], bank[5][0:32, :], ACT.Copy).then_inc(S("glT_ready"), 1)
                act.sem_inc(S("gqk_free"), 4)
                for i in loop(U_GQK, 2):
                    for s in range(2):
                        ahead(U_GQK, i, s)
                        for b in range(2):
                            act.wait_ge(mm, 2 * U_GQK + 4 * i + 2 * s + b + 1)
                            copy(tile(m["gQK"], 4 * i + 2 * s + b), bank[2 * s + b][:, :], S("gqk_free"), scale=1.0 if b else P ** -0.5)
                act.wait_ge(S("gla_in"), 48)
                gv = v3(m["gv"][:, :], NT)
                for hd in loop(U_GV, 4, steps=6):
                    for d in range(2):
                        act.wait_ge(S("gate_mm"), 2 * hd + 1)
                        act.activation(m["wgs"][:, P * d:P * (d + 1)], m["wgf"][:, ds(512 * d + P * hd, P)], ACT.Copy).then_inc(S("wgs_ready"), 1)
                    for s in range(2):
                        ahead(U_GV, hd, s)
                        for hf in range(2):
                            act.wait_ge(mm, 2 * U_GV + 4 * hd + 2 * s + hf + 1)
                            act.wait_ge(S("go_mm"), 4 * hd + 1)
                            copy(gv[:, 2 * hf:2 * hf + 2, 256 * s:256 * s + 256], v3(bank[2 * s + hf][:, :], 2), S("gv_ready"))
                    for d in range(2):
                        lg = tile(m["lg"], d)
                        act.wait_ge(S("gate_mm"), 2 * hd + d + 1 + 1)
                        if d == 0:
                            act.wait_ge(S("att_used"), hd + 1)
                        act.wait_ge(S("kd_turned"), 2 * hd + d + 1)
                        chain(act.activation(lg, bank[d][:, :], ACT.Identity, bias=col("gla_b_gate_2", 4 * d + hd)))
                        chain(act.activation(t32[0][:, :], lg, ACT.Abs))
                        chain(act.activation(t32[0][:, :], t32[0][:, :], ACT.Exp, scale=-1.0))
                        act.activation(t32[0][:, :], t32[0][:, :], ACT.Ln, bias=1.0).then_inc(S("lg_log"), 1)
                        act.wait_ge(S("gcum"), 2 * hd + d + 1)
                        last = v3(t32[1][:, :], NGC)[:, :, (GC - 1) * (1 - d):(GC - 1) * (1 - d) + 1]
                        act.activation(m["gdec"][:, NGC * d:NGC * (d + 1)].unsqueeze(2), last, ACT.Exp, scale=1 / 16).then_inc(S("gdec_ready"), 1)
                        for e, (src, sc) in enumerate(((t32[1], 1 / 16), (t32[1], -1 / 16), (t32[0], 1 / 16))):
                            if e:
                                act.wait_ge(S("g_used"), 6 * hd + 3 * d + e)
                            act.activation(lg, src[:, :], ACT.Exp, scale=sc).then_inc(S("g_exp"), 1)
                        act.wait_ge(S("kd_turned"), 2 * hd + d + 1 + 1)
                        if d == 1:
                            act.wait_ge(S("gu_mm"), 14 * hd + 7 + 1)
                        else:
                            act.wait_ge(S("gu_mm"), 14 * hd + 1)
                        copy(m["kdt"][:, :], bank[6][:, :], S("kdt_ready"))
                    for t in range(NT - 1, -1, -1):
                        act.wait_ge(S("go_mm"), 4 * hd + NT - t + 1)
                        act.activation(v3(m["gO"][:, :], NT)[:, t, ds(512 * hd, 512)], bank[3][:, :], ACT.Copy).then_inc(S("go_copy"), 1)
                        act.wait_ge(S("go_copy"), 4 * hd + NT - t)
                        act.activation(t32[0][:, :], bank[3][:, :], ACT.Square, accum_out=stat[:, ds(4 * t + hd, 1)]).then_inc(S("go_free"), 1)
                        act.wait_ge(S("go_free"), 4 * hd + NT - t + 1)
                act.wait_ge(S("gsq_mean"), 1)
                act.activation(stat[:, 0:16], stat[:, 0:16], ACT.Sqrt).then_inc(S("gsq_root"), 1)
                for i in loop(U_GZ, 4):
                    for s in range(2):
                        ahead(U_GZ, i, s)
                        for hf in range(2):
                            act.wait_ge(mm, 2 * U_GZ + 4 * i + 2 * s + hf + 1)
                            act.wait_ge(S("gz_used"), 4 * i + 2 * s + hf + 1)
                            act.activation(tile(m_gla2["gzs"], hf), bank[2 * s + hf][:, :], ACT.Silu).then_inc(S("gz_ready"), 1)
                for i in loop(U_GLA_OUT, 4):
                    for s in range(2):
                        ahead(U_GLA_OUT, i, s)

            if on("end"):
                norm(7)
            for t in range(NT):
                for k in range(KT):
                    act.wait_ge(S("out_turned"), KT * t + k + 1)
                    copy(m_end["otk"][:, DM * t + P * k:DM * t + P * (k + 1)], bank[k % 4][:, 0:P], S("out_ready"))

        @block.vector
        def _(dve):
            chain = Chain(dve, S("dve_chain"))
            tt, ts, stt3 = dve.tensor_tensor, dve.tensor_scalar, dve.scalar_tensor_tensor

            def norm(j, name, k0=0, to="h"):
                dve.wait_ge(S("sums"), j + 1)
                ts(rstd[:, :], bank[4][:, :], 1.0 / DM, EPS, ALU.mult, ALU.add).then_inc(S("mean_ready"), 1)
                dve.wait_ge(S("root_ready"), j + 1)
                chain(dve.reciprocal(rstd[:, :], rstd[:, :]))
                for k in range(KT):
                    t = t32[k % 2][:, :]
                    if to == "x":
                        stt3(tile(xT, k), tile(xT, k), col(name, k0 + k), rstd[:, :], ALU.mult, ALU.mult).then_inc(res_done, 1)
                        continue
                    chain(stt3(t, tile(xT, k), col(name, k0 + k), rstd[:, :], ALU.mult, ALU.mult))
                    chain(dve.tensor_copy(tile(hHi, k), t))
                    tt(tile(hLo, k), t, tile(hHi, k).bitcast(F32), ALU.subtract).then_inc(h_ready, 1)

            def residual(r, count, per, mark, n_loop, free):
                dve.sem_inc(S(free), count)
                with dve.Fori(0, n_loop) as i:
                    for q in range(per):
                        dve.wait_ge(mm, mark(i, q))
                        x = tile(xT, per * i + q)
                        tt(x, x, bank[q][:, :], ALU.add).then_inc(res_done, 1)
                        dve.wait_ge(res_done, 8 * r + per * i + q + 1)
                        dve.sem_inc(S(free), 1)

            for k in range(KT):
                dve.wait_ge(S("x_turn"), k + 1)
                dve.tensor_copy(tile(xT, k), bank[k % 4][:, :]).then_inc(res_done, 1)
            dve.wait_ge(res_done, 8)
            dve.wait_ge(S("vec_ready"), 2)

            norm(0, "mix_norm")
            cu = m_conv["cu"]
            dve.memset(v3(cu[:, :], KT)[:, :, 0:2], 0.0).then_inc(S("cu_edge"), 1)
            with dve.Fori(0, 4) as i:
                for b in range(2):
                    dve.wait_ge(mm, 4 * i + b + 3)
                    dve.wait_ge(S("c_ready"), 2 * i + b + 1 + 1)
                    tt(cu[:, ds(514 * (2 * i + b) + 2, SEQ)], bank[2 + b][:, :], m_conv[f"c{b}"][:, :], ALU.mult).then_inc(S("cu_done"), 1)
            dve.wait_ge(S("cu_done"), 8 + 1)
            dve.wait_ge(S("cu_edge"), 1)
            dve.sem_inc(S("y_free"), 4)
            with chain.loop(2, 16 + 8) as i:
                for q in range(4):
                    k = 4 * i + q
                    acc = tile(m_conv["cacc"], q % 2)
                    chain(ts(acc, cu[:, ds(514 * k, SEQ)], col("conv_kernel", k), None, ALU.mult))
                    for j in (1, 2):
                        chain(stt3(acc, cu[:, ds(514 * k + j, SEQ)], col("conv_kernel", 8 * j + k), acc, ALU.mult, ALU.add))
                    dve.wait_ge(mm, 2 * U_CONV_B + 4 * i + q + 1)
                    chain(tt(t32[q % 2][:, :], bank[q][:, :], acc, ALU.mult))
                    dve.sem_inc(S("y_free"), 1)
                    chain(dve.tensor_copy(tile(m_conv["yHi"], k), t32[q % 2][:, :]))
                    chain(tt(tile(m_conv["yLo"], k), t32[q % 2][:, :], tile(m_conv["yHi"], k).bitcast(F32), ALU.subtract))
            dve.sem_inc(S("y_ready"), 1)
            residual(R_CONV, 4, 4, lambda i, q: 2 * U_CONV_OUT + 4 * i + q + 1, 2, "conv_free")

            def ffn(j, u_up, u_down):
                norm(2 * j + 1, "ffn_norm", 8 * j)
                f = m_ffn[j]
                aHi, aLo, sil = f[f"f{j}aHi"], f[f"f{j}aLo"], f[f"f{j}sil"]
                with chain.loop(FT // 2, 4) as i:
                    for b in range(2):
                        dve.wait_ge(mm, 2 * u_up + 4 * i + b + 3)
                        dve.wait_ge(S(f"sil_ready{j}"), 2 * i + b + 1 + 1)
                        chain(tt(t32[b][:, :], bank[2 + b][:, :], tile(sil, b), ALU.mult))
                        chain(dve.tensor_copy(tile(aHi, 2 * i + b), t32[b][:, :]))
                        tt(tile(aLo, 2 * i + b), t32[b][:, :], tile(aHi, 2 * i + b).bitcast(F32), ALU.subtract).then_inc(S(f"a_done{j}"), 1)
                residual(2 + 2 * j, 2, 2, lambda i, q: 2 * u_down + 8 * i + 4 * q + 4, 4, f"ffn_free{j}")

            if on("ffn0"):
                ffn(0, U_FFN0, U_DOWN0)

            if on("attn"):
                dve.memset(m_att["rb"][NBUCKETS:NBUCKETS + 1, :], 1.0).then_inc(S("rb_one"), 1)
                norm(2, "mix_norm", 8)
                ast = m_att["ast"]

                def scored(pr, hh):
                    hd = 2 * pr + hh
                    dve.wait_ge(S(f"g_in{hh}"), 16 * (pr + 1))
                    dve.wait_ge(S("prob_turned"), 4 * hd)
                    for n, i in enumerate(S_ORDER):
                        w = P * (i + 1)
                        dve.wait_ge(S("scores"), 4 * hd + max(n + 1, 2))
                        dve.sem_inc(S("scores_seen"), 1)
                        src = [bank[4][:, 0:128], bank[5][:, 0:256], bank[4][:, 128:512], bank[6][:, :]][i]
                        reg = slice(64 * i * (i + 1), 64 * (i + 1) * (i + 2))
                        chain(dve.tensor_tensor_reduce(m_att[f"prob{hh}"][:, reg], src, m_att[f"G{hh}"][:, SEQ - w:SEQ], 1.0, -3e38,
                                                       ALU.add, ALU.max, ast[:, 16 * hh + i:16 * hh + i + 1]))
                        ts(ast[:, 16 * hh + 4 + i:16 * hh + 5 + i], ast[:, 16 * hh + i:16 * hh + i + 1], -1.0, None, ALU.mult)\
                            .then_inc(S("scored"), 1)

                def weighed(pr, hh):
                    hd = 2 * pr + hh
                    dve.wait_ge(S("prob_ready"), 4 * hd + 4)
                    chain(dve.reciprocal(ast[:, 16 * hh + 12:16 * hh + 16], ast[:, 16 * hh + 8:16 * hh + 12]))
                    dve.wait_ge(S("pv"), hd + 1 + 1)
                    tt(v3(m_att["otok"][:, :], NT)[:, :, ds(64 * hd, 64)], v3(bank[7][:, 0:256], NT),
                       bc(ast[:, 16 * hh + 12:16 * hh + 16], 64), ALU.mult).then_inc(S("o_done"), 1)

                scored(0, 0)
                with chain.loop(HEADS // 2 - 1, 10) as pr:
                    scored(pr, 1)
                    weighed(pr, 0)
                    scored(pr + 1, 0)
                    weighed(pr, 1)
                scored(HEADS // 2 - 1, 1)
                weighed(HEADS // 2 - 1, 0)
                weighed(HEADS // 2 - 1, 1)
                for k in range(KT):
                    dve.wait_ge(S("o_turned"), k + 1)
                    o = v3(bank[k % 4][:, :], NT)[:, :, ::-1]
                    chain(dve.tensor_copy(v3(tile(hHi, k), NT), o))
                    tt(v3(tile(hLo, k), NT), o, v3(tile(hHi, k).bitcast(F32), NT), ALU.subtract).then_inc(S("ho_ready"), 1)
                residual(R_ATT, 4, 4, lambda i, q: 2 * U_ATTN_OUT + 4 * i + q + 1, 2, "att_free")

            if on("ffn1"):
                ffn(1, U_FFN1, U_DOWN1)
            if on("mid"):
                norm(4, "final_norm", 0, "x")
                dve.wait_ge(res_done, 8 * (R_MID + 1))
                dve.sem_inc(S("mid_done"), 8)

            if on("ssd"):
                m = m_ssd
                dve.wait_ge(S("ssd_in"), 64)
                chain(dve.tensor_copy(m["wdtHi"][:, :], m["Rm"][:, 0:SEQ]))
                tt(m["wdtLo"][:, :], m["Rm"][:, 0:SEQ], m["wdtHi"][:, :].bitcast(F32), ALU.subtract).then_inc(S("wdt_ready"), 1)
                xpad = v3(m["xpad"][:, :], 4)
                dve.memset(xpad[:, :, 0:2], 0.0).then_inc(S("xpad_edge"), 1)
                dve.memset(xpad[:, :, 514:516], 0.0).then_inc(S("xpad_edge"), 1)
                dve.wait_ge(S("xpad_edge"), 2)
                norm(5, "ssd_norm_2")
                dve.wait_ge(S("dt_mm"), 1)
                tt(v3(m["dt"][:, :], NT), v3(bank[4][:, 0:256], NT), rep(m["dtb"][:, :], NT), ALU.add).then_inc(S("dt_pre"), 1)
                dve.wait_ge(S("dt_log"), 1)
                dve.wait_ge(S("dt_pre"), 1)
                chain(stt3(m["dt"][:, :], m["dt"][:, :], 0.0, m["dtA"][:, :], ALU.max, ALU.add))
                dve.wait_ge(S("a_exp"), 1)
                stt3(v3(m["la"][:, :], NT), v3(m["dt"][:, :], NT), -1.0, rep(m["alog"][:, :], NT), ALU.mult, ALU.mult)\
                    .then_inc(S("la_ready"), 1)
                dve.wait_ge(S("decay_exp"), 3)
                chain(tt(m["wst"][:, :], m["wst"][:, :], m["dt"][:, :], ALU.mult))
                dve.sem_inc(S("wst_ready"), 1)
                dve.wait_ge(S("la_ready"), 1)

                Y = v3(m["sY"][:, :], NT)

                def taps(g, q):
                    ct = 2 * g + q if q < 2 else (16 if q == 2 else 24) + g
                    acc = tile(m["xc"], q)
                    x0 = 516 * q
                    dve.wait_ge(S("xpad_ready"), 4 * g + q + 1)
                    chain(ts(acc, m["xpad"][:, x0:x0 + SEQ], tapcol(0, ct), None, ALU.mult))
                    for j in range(1, 4):
                        chain(stt3(acc, m["xpad"][:, x0 + j:x0 + j + SEQ], tapcol(j, ct), acc, ALU.mult, ALU.add))
                    stt3(acc, m["xpad"][:, x0 + 4:x0 + 4 + SEQ], tapcol(4, ct), acc, ALU.mult, ALU.add).then_inc(S("tap_done"), 1)

                def group(g, more):
                    dve.wait_ge(S("cb_mm"), g + 1)
                    for d, mask in enumerate((LE, GE)):
                        chain.note(tt(v3(tile(m["CB"], d), NT), v3(bank[7][:, :], NT), rep(mask[:, :], NT), ALU.mult))
                    for step in range(3):
                        bufs = []
                        for d in range(2):
                            c = ssd_chunk(step, d)
                            at = 1024 * d + 256 * (c + 1 - 2 * d)
                            bufs.append(m["stt"][:, at:at + 256])
                            if step:
                                chain.note(tt(h4(bufs[d]), h4(m["stt"][:, 1024 * d + 256 * c:1024 * d + 256 * c + 256]),
                                              bc(heads("etot", c, d, g), 64), ALU.mult))
                        for d in range(2):
                            dve.wait_ge(S("state_mm"), 6 * g + 2 * step + d + 1)
                            if step:
                                if d == 0:
                                    dve.wait_ge(chain.sem, chain.n + chain.extra)
                                chain.note(tt(bufs[d], bufs[d], bank[4 + d][:, 0:256], ALU.add))
                            else:
                                chain.note(dve.tensor_copy(bufs[d], bank[4 + d][:, 0:256]))
                        dve.wait_ge(chain.sem, chain.n + chain.extra)
                        dve.sem_inc(S("state_ready"), 1)
                    for c in range(NT):
                        for d in range(2):
                            MT = tile(m["MT"], 2 * (c % 2) + d)
                            dve.wait_ge(S("ex_ready"), 8 * g + 2 * c + d + 1)
                            tt(v3(MT, HPG), v3(MT, HPG), rep(m["CB"][:, SEQ * d + P * c:SEQ * d + P * c + P], HPG),
                               ALU.mult).then_inc(S("mt_ready"), 1)
                        xd, yt = m["xd"][:, :], m["yt"]
                        tt(h4(xd), h4(m["xt"][:, 256 * c:256 * c + 256]), bc(m["dsk"][:, ds(HPG * g, HPG)], 64), ALU.mult)\
                            .then_inc(S("skip_ready"), 1)
                        if more:
                            if c == 3:
                                dve.wait_ge(S("c_read"), g + 1)
                            taps(g + 1, c)
                        dve.wait_ge(S("y_mm"), 4 * g + c + 1)
                        dirs = [d for d in range(2) if not (c == 0 and d == 0) and not (c == 3 and d == 1)]
                        for d in dirs:
                            chain.note(tt(h4(yt[:, 256 * d:256 * d + 256]), h4(bank[7][:, 256 * d:256 * d + 256]), bc(heads("ecum", c, d, g), 64), ALU.mult))
                        dve.wait_ge(S("skip_ready"), 4 * g + c + 1 + 1)
                        chain(tt(xd, xd, bank[6][:, 0:256], ALU.add))
                        dve.sem_inc(S("y_bank_free"), 1)
                        if len(dirs) == 2:
                            chain(tt(xd, xd, yt[:, 0:256], ALU.add))
                        chain(tt(Y[:, c, ds(256 * g, 256)], xd, yt[:, 256 * dirs[-1]:256 * dirs[-1] + 256], ALU.add))

                for q in range(4):
                    taps(0, q)
                g_steps = 2 + (2 + 4 + 4) + 4 * 4 + (3 + 5 + 5 + 3)
                with chain.loop(SSD_GROUPS - 1, g_steps) as g:
                    group(g, True)
                group(SSD_GROUPS - 1, False)
                with chain.loop(4, 4) as i:
                    for s in range(2):
                        for hf in range(2):
                            dve.wait_ge(S("sz_ready"), 4 * i + 2 * s + hf + 1 + 1)
                            y = Y[:, 2 * hf:2 * hf + 2, ds(512 * i + 256 * s, 256)]
                            chain(tt(y, y, v3(tile(m_ssd2["szs"], hf), 2), ALU.mult))
                            dve.sem_inc(S("sz_used"), 1)
                dve.wait_ge(S("sz_squared"), 32 + 1)
                ts(stat[:, 0:32], stat[:, 0:32], 1.0 / 256, EPS, ALU.mult, ALU.add).then_inc(S("ssq_mean"), 1)
                dve.wait_ge(S("ssq_root"), 1)
                chain(dve.reciprocal(stat[:, 0:32], stat[:, 0:32]))
                for part, (Hi, Lo) in enumerate(((hHi, hLo), (m_ssd2["sHi"], m_ssd2["sLo"]))):
                    with chain.loop(4, 4) as i:
                        for b in range(2):
                            k = 2 * i + b
                            dve.wait_ge(S("sy_turned"), 8 * part + 2 * i + 1)
                            tt(v3(t32[b][:, :], NT), Y[:, :, ds(DM * part + P * k, P)],
                               v3(stat[:, 0:32], NT)[:, :, ds(4 * part + i, 1)].broadcast_to([P, NT, P]),
                               ALU.mult).then_inc(S("sy_scaled"), 1)
                        for b in range(2):
                            k = 2 * i + b
                            g = col("ssd_gnorm_2", 8 * part + k)
                            dve.wait_ge(S("sy_turned"), 8 * part + 2 * i + b + 1 + 1)
                            chain(ts(tile(Hi, k), bank[b][:, :], g, None, ALU.mult))
                            chain(stt3(tile(Lo, k), bank[b][:, :], g, tile(Hi, k).bitcast(F32), ALU.mult, ALU.subtract))
                dve.sem_inc(S("sy_ready"), 1)
                residual(R_SSD, 2, 2, lambda i, q: 2 * U_SSD_OUT + 4 * i + 2 * q + 2, 4, "ssd_free")

            if on("gla"):
                m = m_gla
                dve.memset(m["wgf"][:, :], 0.0).then_inc(S("wgf_zero"), 1)
                chain(dve.tensor_copy(m["mF"][:, :], LE[:, :]))
                chain(dve.memset(m["mF"][0:GC, GC:P], 0.0))
                chain(dve.tensor_copy(m["mB"][:, :], GE[:, :]))
                chain(dve.memset(m["mB"][GC:P, 0:GC], 0.0))
                chain(dve.memset(m["attF"][:, :], 0.0))
                chain(dve.memset(m["attB"][:, :], 0.0))
                chain(dve.memset(m["m64"][:, :], 1.0))
                chain(dve.memset(v3(m["m64"][:, :], NGC)[:, :, 0:1], 0.0))
                dve.wait_ge(S("gla_in"), 48)
                chain(dve.tensor_copy(m_gl["wglHi"][:, :], m_gla["kg"][:, 0:256]))
                tt(m_gl["wglLo"][:, :], m_gla["kg"][:, 0:256], m_gl["wglHi"][:, :].bitcast(F32), ALU.subtract).then_inc(S("wgl_ready"), 1)
                dve.wait_ge(S("wgl_ready"), 1)
                norm(6, "gla_norm_2")
                dve.wait_ge(S("gqk_free"), 4 + 8)

                def chunkless(ap):
                    return v3(ap, NGC)

                def gla_head(hd):
                    q, k = tile(m["gQK"], 2 * hd), tile(m["gQK"], 2 * hd + 1)
                    cum, diff = t32[1][:, :], t32[0][:, :]
                    for d in range(2):
                        lg = tile(m["lg"], d)
                        dve.wait_ge(S("lg_log"), 2 * hd + d + 1)
                        chain(stt3(lg, lg, 0.0, diff, ALU.min, ALU.subtract))
                        if d == 0:
                            chain(dve.tensor_tensor_scan(cum, m["m64"][:, :], lg, 0.0, ALU.mult, ALU.add))
                        else:
                            chain(dve.tensor_tensor_scan(cum[:, ::-1], m["m64"][:, :], lg[:, ::-1], 0.0, ALU.mult, ALU.add))
                        at = (GC - 1) * (1 - d)
                        last = chunkless(cum)[:, :, at:at + 1].broadcast_to([P, NGC, GC])
                        chain(tt(chunkless(diff), last, chunkless(cum), ALU.subtract))
                        dve.sem_inc(S("gcum"), 1)
                        dve.wait_ge(S("g_exp"), 6 * hd + 3 * d + 1)
                        tt(tile(m["qg"], d), q, lg, ALU.mult).then_inc(S("g_used"), 1)
                        dve.wait_ge(S("g_exp"), 6 * hd + 3 * d + 2)
                        tt(tile(m["kg"], d), k, lg, ALU.mult).then_inc(S("g_used"), 1)
                        dve.wait_ge(S("g_exp"), 6 * hd + 3 * d + 3)
                        tt(diff, k, lg, ALU.mult).then_inc(S("g_used"), 1)
                        dve.wait_ge(S("gdec_ready"), 2 * hd + d + 1)
                        if d == 0:
                            for c in range(7):
                                dve.wait_ge(S("gu_mm"), 14 * hd + c + 1 + 1)
                                new = tile(m["gst"], c + 1)
                                src = bank[4 + c % 2][:, :]
                                if c:
                                    ins = stt3(new, tile(m["gst"], c), m["gdec"][:, c:c + 1], src, ALU.mult, ALU.add)
                                else:
                                    ins = dve.tensor_copy(new, src)
                                ins.then_inc(S("gs_ready"), 1)
                                dve.wait_ge(S("gs_ready"), 14 * hd + c + 1 + 1)
                    att = tile(m["lg"], 0)
                    for t in range(NT):
                        dve.wait_ge(S("gatt_mm"), 2 * hd + 2)
                        dve.sem_inc(S("gatt_seen"), 1)
                        dve.copy_predicated(m["attF"][:, :], m["mF"][:, :].bitcast(I32), bank[7][:, P * t:P * (t + 1)]).then_inc(S("attF_ready"), 1)
                        chain(dve.copy_predicated(m["attB"][:, :], m["mB"][:, :].bitcast(I32), bank[2][:, P * t:P * (t + 1)]))
                        dve.wait_ge(S("attF_ready"), 4 * hd + t + 1)
                        chain(tt(att[:, P * t:P * (t + 1)], m["attF"][:, :], m["attB"][:, :], ALU.add))
                    dve.sem_inc(S("att_ready"), 1)
                    for e in range(7):
                        c = 7 - e
                        dve.wait_ge(S("gu_mm"), 14 * hd + 7 + e + 1 + 1)
                        new, old = tile(m["gsb"], (c - 1) % 2), tile(m["gsb"], c % 2)
                        src = bank[4 + e % 2][:, :]
                        dve.wait_ge(S("go_mm"), 4 * hd + NT - (c + 1) // 2 + 1)
                        if e:
                            ins = stt3(new, old, m["gdec"][:, NGC + c:NGC + c + 1], src, ALU.mult, ALU.add)
                        else:
                            ins = dve.tensor_copy(new, src)
                        ins.then_inc(S("gs_ready"), 1)
                        dve.wait_ge(S("gs_ready"), 14 * hd + 7 + e + 1 + 1)

                with chain.loop(4, 6 + 8) as hd:
                    gla_head(hd)
                dve.wait_ge(S("go_free"), 16 + 1)
                ts(stat[:, 0:16], stat[:, 0:16], 1.0 / 512, EPS, ALU.mult, ALU.add).then_inc(S("gsq_mean"), 1)
                dve.wait_ge(S("gsq_root"), 1)
                chain(dve.reciprocal(stat[:, 0:16], stat[:, 0:16]))
                O = v3(m["gO"][:, :], NT)
                with dve.Fori(0, 4) as i:
                    for s in range(2):
                        for hf in range(2):
                            dve.wait_ge(S("gz_ready"), 4 * i + 2 * s + hf + 1 + 1)
                            for e in range(2):
                                o = O[:, 2 * hf + e, ds(512 * i + 256 * s, 256)]
                                ins = stt3(o, o, stat[:, ds(4 * (2 * hf + e) + i, 1)], m_gla2["gzs"][:, SEQ * hf + 256 * e:SEQ * hf + 256 * e + 256],
                                           ALU.mult, ALU.mult).then_inc(S("gate_half"), 1)
                            dve.wait_ge(S("gate_half"), 8 * i + 4 * s + 2 * hf + 2)
                            dve.sem_inc(S("gz_used"), 1)
                for part, (Hi, Lo) in enumerate(((hHi, hLo), (m_gla2["gHi"], m_gla2["gLo"]))):
                    with chain.loop(2, 8) as i:
                        for q in range(4):
                            b = q % 2
                            k = 4 * i + q
                            dve.wait_ge(S("gy_turned"), 8 * part + 4 * i + (q - q % 2) + 1)
                            dve.tensor_copy(v3(t32[b][:, :], NT), O[:, :, ds(DM * part + P * k, P)]).then_inc(S("gy_scaled"), 1)
                            if b == 0:
                                continue
                            for bb in range(2):
                                k2 = 4 * i + q - 1 + bb
                                g = col("gla_onorm_2", q - 1 + bb)
                                dve.wait_ge(S("gy_turned"), 8 * part + 4 * i + q + bb + 1)
                                chain(ts(tile(Hi, k2), bank[bb][:, :], g, None, ALU.mult))
                                chain(stt3(tile(Lo, k2), bank[bb][:, :], g, tile(Hi, k2).bitcast(F32), ALU.mult, ALU.subtract))
                dve.sem_inc(S("gy_ready"), 1)
                residual(R_GLA, 2, 2, lambda i, q: 2 * U_GLA_OUT + 4 * i + 2 * q + 2, 4, "gla_free")

            if on("end"):
                norm(7, "final_norm_2", 0, "x")
                dve.wait_ge(res_done, 8 * 9)

        @block.tensor
        def _(pe):
            def mark(ins):
                ins.then_inc(mm, 1)

            def product(dst, hi1, lo1, hi2, lo2, first, last):
                pe.matmul(dst, hi1, hi2, start=first, stop=False)
                pe.matmul(dst, hi1, lo2, start=False, stop=False)
                return pe.matmul(dst, lo1, hi2, start=False, stop=last)

            def chan(dst, s, at, Hi, Lo, ks, first=True, last=True, x0=0):
                for n, k in enumerate(ks):
                    w = slice(at(k), at(k) + P)
                    x = slice(SEQ * (k + x0), SEQ * (k + x0 + 1))
                    ins = product(dst, whi[s][:, w], wlo[s][:, w], Hi[:, x], Lo[:, x], first and n == 0, last and n == len(ks) - 1)
                return ins

            def tokens(s, hf, dst):
                for e in range(2):
                    for k in range(KT):
                        x = slice(SEQ * k + P * (2 * hf + e), SEQ * k + P * (2 * hf + e + 1))
                        w = slice(256 * k, 256 * k + 256)
                        ins = product(dst[:, 256 * e:256 * e + 256], hHi[:, x], hLo[:, x], whi[s][:, w], wlo[s][:, w], k == 0, k == KT - 1)
                return ins

            def unit(n):
                pe.wait_ge(w_lo, n + 1)

            def norm(j):
                for k in range(KT):
                    pe.wait_ge(S("sq_ready"), 8 * j + k + 1)
                    ins = pe.matmul(bank[4][:, :], ones[:, :], t32[k % 2][:, :], start=(k == 0), stop=(k == KT - 1))
                    ins.then_inc(S("sq_used"), 1)
                pe.wait_ge(S("sq_used"), 8 * j + 8)
                pe.sem_inc(S("sums"), 1)
                pe.wait_ge(h_ready, 8 * (j + 1 - (j > 4))) if j not in (4, 7) else None

            pair = lambda b: (lambda k: 256 * k + P * b)

            pe.wait_ge(S("cst"), 11)
            pe.wait_ge(S("vec_in"), 16 * (len(VEC_ROWS) + 3))
            vr = m_in["vrows"]
            pe.transpose(bank[4][:, 0:NVEC], vr[0:NVEC, 0:P], ident[0:NVEC, 0:NVEC]).then_inc(S("vec_turned"), 1)
            pe.transpose(bank[4][:, P:2 * P], vr[:, P:2 * P], ident[:, :]).then_inc(S("vec_turned"), 1)
            pe.transpose(bank[4][:, 2 * P:2 * P + 64], vr[0:64, 2 * P:3 * P], ident[0:64, 0:64]).then_inc(S("vec_turned"), 1)
            pe.wait_ge(S("x_in"), 16)
            for k in range(KT):
                if k >= 4:
                    pe.wait_ge(res_done, k - 3)
                for t in range(NT):
                    ins = pe.transpose(bank[k % 4][:, P * t:P * (t + 1)], m_in["xtok"][:, DM * t + P * k:DM * t + P * (k + 1)], ident[:, :])
                ins.then_inc(S("x_turn"), 1)
            pe.wait_ge(S("vec_ready"), 2)
            norm(0)

            with pe.Fori(0, 4) as i:
                for s in range(2):
                    unit(2 * i + s)
                    pe.wait_ge(S("cu_done" if s else "c_ready"), 2 * i + 1)
                    for b in range(2):
                        mark(chan(bank[2 * s + b][:, :], s, pair(b), hHi, hLo, range(KT)))
            pe.wait_ge(S("cu_done"), 8 + 1)
            with pe.Fori(0, 2) as i:
                for s in range(2):
                    unit(U_CONV_B + 2 * i + s)
                    for b in range(2):
                        pe.wait_ge(S("y_free"), 4 * i + 2 * s + b + 1)
                        mark(chan(bank[2 * s + b][:, :], s, pair(b), hHi, hLo, range(KT)))

            def out8(u0, free, Hi, Lo):
                with pe.Fori(0, 2) as i:
                    for s in range(2):
                        unit(u0 + 2 * i + s)
                        for b in range(2):
                            pe.wait_ge(S(free), 4 * i + 2 * s + b + 1)
                            mark(chan(bank[2 * s + b][:, :], s, pair(b), Hi, Lo, range(KT)))

            def out16(u0, free, Hi, Lo):
                with pe.Fori(0, 4) as i:
                    for s in range(2):
                        unit(u0 + 2 * i + s)
                        pe.wait_ge(S(free), 2 * i + s + 1)
                        mark(chan(bank[s][:, :], s, lambda k: P * k, hHi, hLo, range(8), True, False))
                        mark(chan(bank[s][:, :], s, lambda k: P * k, Hi, Lo, range(8, 16), False, True, x0=-8))

            pe.wait_ge(S("y_ready"), 1)
            out8(U_CONV_OUT, "conv_free", m_conv["yHi"], m_conv["yLo"])

            def ffn(j, u_up, u_down):
                norm(2 * j + 1)
                aHi, aLo = m_ffn[j][f"f{j}aHi"], m_ffn[j][f"f{j}aLo"]
                with pe.Fori(0, FT // 2) as i:
                    for s in range(2):
                        unit(u_up + 2 * i + s)
                        pe.wait_ge(S(f"a_done{j}" if s else f"sil_ready{j}"), 2 * i + 1)
                        for b in range(2):
                            mark(chan(bank[2 * s + b][:, :], s, pair(b), hHi, hLo, range(KT)))
                pe.wait_ge(S(f"a_done{j}"), FT + 1)
                with pe.Fori(0, 4) as i:
                    for q in range(2):
                        pe.wait_ge(S(f"ffn_free{j}"), 2 * i + q + 1)
                        for s in range(2):
                            unit(u_down + 4 * i + 2 * q + s)
                            ks = range(HALF_FFN * s, HALF_FFN * (s + 1))
                            at = lambda k: P * (k - HALF_FFN * s)
                            mark(chan(bank[q][:, :], s, at, aHi, aLo, ks[:5], s == 0, False))
                            mark(chan(bank[q][:, :], s, at, aHi, aLo, ks[5:], False, s == 1))

            if on("ffn0"):
                ffn(0, U_FFN0, U_DOWN0)

            if on("attn"):
                pe.wait_ge(S("bias_in"), 32)
                pe.wait_ge(S("rb_one"), 1)
                pe.matmul(bank[5][0:HEADS, :], m_att["rb"][:, :], m_att["bkt"][:, 0:SEQ], start=True, stop=True).then_inc(S("toe_mm"), 1)
                pe.matmul(bank[6][0:HEADS, 0:P], m_att["rb"][:, :], m_att["bkt"][:, SEQ:640], start=True, stop=True).then_inc(S("toe_mm"), 1)
                norm(2)
                with pe.Fori(0, 4) as i:
                    for s in range(2):
                        unit(U_QKV + 2 * i + s)
                        for b in range(2):
                            pe.wait_ge(S("qkv_free"), 4 * i + 2 * s + b + 1)
                            mark(chan(bank[2 * s + b][:, :], s, pair(b), hHi, hLo, range(KT)))
                with pe.Fori(0, 2) as i:
                    for s in range(2):
                        unit(U_QKV + 8 + 2 * i + s)
                        for hf in range(2):
                            pe.wait_ge(S("qkv_free"), 16 + 4 * i + 2 * s + hf + 1)
                            mark(tokens(s, hf, bank[2 * s + hf]))

                def scores(pr, hh):
                    hd = 2 * pr + hh
                    rows = slice(64 * hh, 64 * hh + 64)
                    pe.wait_ge(S("qs_ready"), 2 * pr + 2)
                    pe.wait_ge(S("scored"), 4 * hd)
                    for i in S_ORDER:
                        w = P * (i + 1)
                        dst = [bank[4][:, 0:128], bank[5][:, 0:256], bank[4][:, 128:512], bank[6][:, :]][i]
                        pe.matmul(dst, m_att["qS"][rows, P * i:P * (i + 1)], m_att["kS"][rows, 0:w], start=True, stop=True)\
                            .then_inc(S("scores"), 1)

                def weigh(pr, hh):
                    hd = 2 * pr + hh
                    prob, pT = m_att[f"prob{hh}"], m_att["pT"]
                    pe.wait_ge(S("prob_ready"), 4 * hd + 4)
                    pe.wait_ge(S("pt_ready"), 4 * hd + 1)
                    for j in range(NT):
                        for i in range(j, NT):
                            at = 64 * i * (i + 1) + P * j
                            ins = pe.transpose(bank[j][:, P * (i - j):P * (i - j + 1)], prob[:, at:at + P], ident[:, :])
                        ins.then_inc(S("prob_turned"), 1)
                    pe.wait_ge(S("pt_ready"), 4 * hd + 4 + 1)
                    pe.wait_ge(S("o_done"), hd + 1)
                    for i in range(NT):
                        for j in range(i + 1):
                            at = [0, 512, 896, 1152][j] + P * (i - j)
                            ins = pe.matmul(bank[7][:, 64 * i:64 * i + 64], pT[:, at:at + P], m_att["vtok"][:, ds(DM * j + 64 * hd, 64)],
                                            start=(j == 0), stop=(j == i))
                    ins.then_inc(S("pv"), 1)

                pe.wait_ge(S("qkv_free"), 4 + 16 + 8)
                scores(0, 0)
                with pe.Fori(0, HEADS // 2 - 1) as pr:
                    scores(pr, 1)
                    weigh(pr, 0)
                    scores(pr + 1, 0)
                    weigh(pr, 1)
                scores(HEADS // 2 - 1, 1)
                weigh(HEADS // 2 - 1, 0)
                weigh(HEADS // 2 - 1, 1)
                pe.wait_ge(S("o_done"), HEADS + 1)
                for k in range(KT):
                    if k >= 4:
                        pe.wait_ge(S("ho_ready"), k - 3)
                    for t in range(NT):
                        ins = pe.transpose(bank[k % 4][:, P * t:P * (t + 1)], m_att["otok"][:, DM * t + P * k:DM * t + P * (k + 1)], ident[:, :])
                    ins.then_inc(S("o_turned"), 1)
                pe.wait_ge(S("ho_ready"), 8)
                out8(U_ATTN_OUT, "att_free", hHi, hLo)

            if on("ffn1"):
                ffn(1, U_FFN1, U_DOWN1)
            if on("mid"):
                norm(4)

            if on("ssd"):
                m = m_ssd
                norm(5)
                pe.wait_ge(S("wdt_ready"), 1)
                for c in range(NT):
                    for k in range(KT):
                        x = slice(SEQ * k + P * c, SEQ * k + P * (c + 1))
                        w = slice(64 * k, 64 * k + 64)
                        ins = product(bank[4][:, 64 * c:64 * c + 64], hHi[:, x], hLo[:, x], m["wdtHi"][:, w], m["wdtLo"][:, w], k == 0, k == KT - 1)
                ins.then_inc(S("dt_mm"), 1)
                pe.wait_ge(S("la_ready"), 1)
                for c in range(NT):
                    for d in range(2):
                        w = slice(64 * c + 32 * d, 64 * c + 32 * d + 32)
                        for b, mat in ((5, (LE, GE)[d]), (6, (GT, LT)[d]), (7, ones)):
                            ins = pe.matmul(bank[b][:, w], mat[:, :], m["la"][:, w], start=True, stop=True)
                ins.then_inc(S("decays"), 1)
                pe.wait_ge(S("decay_exp"), 3)
                pe.wait_ge(S("xpad_edge"), 2)

                def project(g, q):
                    if q % 2 == 0:
                        unit(U_XBC + 2 * g + q // 2)
                    mark(chan(bank[q][:, :], q // 2, pair(q % 2), hHi, hLo, range(KT)))

                def segments(g, c, d):
                    pe.wait_ge(S("rm_ready"), 8 * g + 2 * c + d + 1)
                    pe.matmul(bank[4 + d][:, :], (GT, LT)[d][:, :], m["Rm"][:, SEQ * d:SEQ * (d + 1)], start=True, stop=True).then_inc(S("seg"), 1)

                def group(g, more):
                    xc, bt = m["xc"], m["bt"]
                    BT, CT = tile(xc, 2), tile(xc, 3)
                    pe.wait_ge(S("xc_ready"), 4 * g + 2)
                    for b in range(2):
                        for e in range(2):
                            for q in range(2):
                                c = 2 * b + e
                                ins = pe.transpose(bank[4 + b][:, 256 * e + P * q:256 * e + P * (q + 1)], xc[:, SEQ * q + P * c:SEQ * q + P * (c + 1)], ident[:, :])
                        ins.then_inc(S("x_turned"), 1)
                    pe.wait_ge(S("xc_ready"), 4 * g + 4)
                    pe.wait_ge(S("y_bank_free"), 4 * g + 1)
                    for c in range(NT):
                        ins = pe.transpose(bank[6][:, P * c:P * (c + 1)], BT[:, P * c:P * (c + 1)], ident[:, :])
                    ins.then_inc(S("x_turned"), 1)
                    for c in range(NT):
                        ins = pe.matmul(bank[7][:, P * c:P * (c + 1)], BT[:, P * c:P * (c + 1)], CT[:, P * c:P * (c + 1)], start=True, stop=True)
                    ins.then_inc(S("cb_mm"), 1)
                    if more:
                        project(g + 1, 0)
                    pe.wait_ge(S("xt_ready"), 3 * g + 3)
                    for step in range(3):
                        if step:
                            pe.wait_ge(S("state_ready"), 3 * g + step)
                        for d in range(2):
                            c = ssd_chunk(step, d)
                            pe.wait_ge(S("xw_ready"), 6 * g + 2 * step + d + 1)
                            pe.matmul(bank[4 + d][:, 0:256], bt[:, P * c:P * (c + 1)], xw_buf(step, d), start=True, stop=True).then_inc(S("state_mm"), 1)
                    pe.wait_ge(S("state_ready"), 3 * g + 3)
                    for d in range(2):
                        segments(g, 0, d)
                    for c in range(NT):
                        if more and c < 3:
                            project(g + 1, c + 1)
                        pe.wait_ge(S("y_bank_free"), 4 * g + c + 1)
                        for d in range(2):
                            if not (c == 0 and d == 0) and not (c == 3 and d == 1):
                                ins = pe.matmul(bank[7][:, 256 * d:256 * d + 256], CT[:, P * c:P * (c + 1)], m["stt"][:, 1024 * d + 256 * c:1024 * d + 256 * c + 256],
                                                start=True, stop=True)
                        if c == 3:
                            ins.then_inc(S("c_read"), 1)
                        else:
                            for d in range(2):
                                pe.wait_ge(S("ex_ready"), 8 * g + 2 * c + d + 1)
                                segments(g, c + 1, d)
                        pe.wait_ge(S("xdt_ready"), 8 * g + 2 * c + 2)
                        pe.wait_ge(S("mt_ready"), 8 * g + 2 * c + 2)
                        for h in range(HPG):
                            for d in range(2):
                                at = 2 * (c % 2) + d
                                ins = pe.matmul(bank[6][:, 64 * h:64 * h + 64], m["MT"][:, SEQ * at + P * h:SEQ * at + P * (h + 1)],
                                                m["xdt"][:, 256 * at + 64 * h:256 * at + 64 * h + 64], start=(d == 0), stop=(d == 1))
                        ins.then_inc(S("y_mm"), 1)

                for q in range(4):
                    project(0, q)
                with pe.Fori(0, SSD_GROUPS - 1) as g:
                    group(g, True)
                group(SSD_GROUPS - 1, False)
                with pe.Fori(0, 4) as i:
                    for s in range(2):
                        unit(U_SZ + 2 * i + s)
                        pe.wait_ge(S("sz_ready"), 4 * i + 0 + 1)
                        for hf in range(2):
                            mark(tokens(s, hf, bank[2 * s + hf]))
                def turn(part, i, b, name):
                    pe.wait_ge(S(name + "_scaled"), 8 * part + 2 * i + b + 1)
                    for t in range(NT):
                        ins = pe.transpose(bank[b][:, P * t:P * (t + 1)], t32[b][:, P * t:P * (t + 1)], ident[:, :])
                    ins.then_inc(S(name + "_turned"), 1)
                with pe.Fori(0, 8) as i:
                    for b in range(2):
                        turn(0, i, b, "sy")
                pe.wait_ge(S("sy_ready"), 1)
                out16(U_SSD_OUT, "ssd_free", m_ssd2["sHi"], m_ssd2["sLo"])

            if on("gla"):
                m = m_gla
                norm(6)
                pe.wait_ge(S("wgl_ready"), 1)
                for t in range(NT):
                    for k in range(KT):
                        x = slice(SEQ * k + P * t, SEQ * k + P * (t + 1))
                        w = slice(32 * k, 32 * k + 32)
                        ins = product(bank[4][:, 32 * t:32 * t + 32], hHi[:, x], hLo[:, x], m_gl["wglHi"][:, w], m_gl["wglLo"][:, w], k == 0, k == KT - 1)
                ins.then_inc(S("gl_mm"), 1)
                pe.wait_ge(S("gl_ready"), 1)
                for t in range(NT):
                    ins = pe.transpose(bank[5][0:32, P * t:P * (t + 1)], m_gl["gl"][:, 32 * t:32 * t + 32], ident[:, :])
                ins.then_inc(S("gl_turned"), 1)
                with pe.Fori(0, 2) as i:
                    for s in range(2):
                        unit(U_GQK + 2 * i + s)
                        for b in range(2):
                            pe.wait_ge(S("gqk_free"), 4 * i + 2 * s + b + 1)
                            mark(chan(bank[2 * s + b][:, :], s, pair(b), hHi, hLo, range(KT)))
                pe.wait_ge(S("gqk_free"), 4 + 8)
                pe.wait_ge(S("glT_ready"), 1)
                gv = m["gv"]
                with pe.Fori(0, 4) as hd:
                    for s in range(2):
                        unit(U_GV + 2 * hd + s)
                        pe.wait_ge(S("gv_ready"), 4 * hd + 1)
                        pe.wait_ge(S("go_free"), 4 * hd + 1)
                        pe.wait_ge(S("att_ready"), hd + 1)
                        for hf in range(2):
                            mark(tokens(s, hf, bank[2 * s + hf]))
                    pe.wait_ge(S("gs_ready"), 14 * hd + 1)
                    pe.wait_ge(S("gv_ready"), 4 * hd + 4 + 1)
                    for d in range(2):
                        pe.wait_ge(S("wgs_ready"), 2 * hd + d + 1)
                        pe.matmul(bank[d][:, :], m["wgs"][:, P * d:P * (d + 1)], rstd[0:32, :], start=True, stop=True).then_inc(S("gate_mm"), 1)

                    def increment(n, c):
                        r, t = c % 2, c // 2
                        if n >= 2:
                            pe.wait_ge(S("gs_ready"), 14 * hd + n - 1 + 1)
                        pe.matmul(bank[4 + (n % 7) % 2][:, :], m["kdt"][GC * r:GC * (r + 1), P * t:P * (t + 1)],
                                  gv[GC * r:GC * (r + 1), SEQ * t:SEQ * (t + 1)], start=True, stop=True).then_inc(S("gu_mm"), 1)

                    for d in range(2):
                        pe.wait_ge(S("g_used"), 6 * hd + 3 * d + 3)
                        pe.wait_ge(S("kdt_ready"), 2 * hd + d + 1)
                        for t in range(NT):
                            ins = pe.transpose(bank[6][:, P * t:P * (t + 1)], t32[0][:, P * t:P * (t + 1)], ident[:, :])
                        ins.then_inc(S("kd_turned"), 1)
                        for t in range(NT):
                            x = slice(SEQ * d + P * t, SEQ * d + P * (t + 1))
                            ins = pe.matmul(bank[2 if d else 7][:, P * t:P * (t + 1)], m["kg"][:, x], m["qg"][:, x], start=True, stop=True)
                        ins.then_inc(S("gatt_mm"), 1)
                        pe.wait_ge(S("kdt_ready"), 2 * hd + d + 1 + 1)
                        if d == 0:
                            for c in range(7):
                                increment(c, c)
                    pe.wait_ge(S("att_ready"), hd + 1 + 1)
                    n = 7
                    for t in range(NT - 1, -1, -1):
                        for c in (2 * t + 2, 2 * t + 1):
                            if c <= 7:
                                pe.wait_ge(S("gs_ready"), 14 * hd + n + 1)
                                increment(n, c)
                                n += 1
                        pe.wait_ge(S("gs_ready"), 14 * hd + n + 1)
                        if t < NT - 1:
                            pe.wait_ge(S("go_free"), 4 * hd + NT - 1 - t + 1)
                        pe.matmul(bank[3][:, :], tile(m["lg"], 0)[:, P * t:P * (t + 1)], gv[:, SEQ * t:SEQ * (t + 1)], start=True, stop=False, skip_group_check=True)
                        for r in range(2):
                            c = 2 * t + r
                            terms = ([(0, tile(m["gst"], c))] if c else []) + ([(1, tile(m["gsb"], c % 2))] if c < 7 else [])
                            for d, state in terms:
                                ins = pe.matmul(bank[3][GC * r:GC * (r + 1), :], m["qg"][:, SEQ * d + GC * c:SEQ * d + GC * (c + 1)], state,
                                                start=False, stop=(d == terms[-1][0]), skip_group_check=True)
                        ins.then_inc(S("go_mm"), 1)
                    pe.wait_ge(S("go_mm"), 4 * hd + 4 + 1)
                    pe.sem_inc(S("att_used"), 1)
                with pe.Fori(0, 4) as i:
                    for s in range(2):
                        unit(U_GZ + 2 * i + s)
                        pe.wait_ge(S("gz_ready"), 4 * i + 1)
                        pe.wait_ge(S("go_free"), 16 + 1)
                        for hf in range(2):
                            mark(tokens(s, hf, bank[2 * s + hf]))
                with pe.Fori(0, 8) as i:
                    for b in range(2):
                        pe.wait_ge(S("gy_scaled"), 2 * i + b + 1)
                        for t in range(NT):
                            ins = pe.transpose(bank[b][:, P * t:P * (t + 1)], t32[b][:, P * t:P * (t + 1)], ident[:, :])
                        ins.then_inc(S("gy_turned"), 1)
                pe.wait_ge(S("gy_ready"), 1)
                out16(U_GLA_OUT, "gla_free", m_gla2["gHi"], m_gla2["gLo"])

            if on("end"):
                norm(7)
            final = 8 * ((last_r + 1) if stages[-1] != "end" else 9)
            pe.wait_ge(res_done, final)
            for t in range(NT):
                for k in range(KT):
                    if KT * t + k >= 4:
                        pe.wait_ge(S("out_ready"), KT * t + k - 3)
                    pe.transpose(bank[k % 4][:, 0:P], xT[:, SEQ * k + P * t:SEQ * k + P * (t + 1)], ident[:, :]).then_inc(S("out_turned"), 1)


def kernel(**inputs):
    import numpy as _np
    import concourse.bacc as _bacc
    from concourse import mybir as _mybir
    from concourse.bass_utils import run_bass_kernel_spmd as _run

    nc = _bacc.Bacc("TRN2", target_bir_lowering=False, num_devices=1)
    arrays, aps = {}, {}
    given = {n: _np.ascontiguousarray(inputs[n]) for n in INPUTS}
    given["bucket_rows"] = bucket_rows()
    for name, a in given.items():
        arrays[f"in_{name}"] = a
        aps[name] = nc.dram_tensor(f"in_{name}", a.shape, _mybir.dt.from_np(a.dtype), kind="ExternalInput").ap()
    out = nc.dram_tensor("out_x", (1, SEQ, DM), F32, kind="ExternalOutput").ap()
    build(nc, aps, out)
    r = _run(nc, [arrays], core_ids=[0])
    return r.results[0]["out_x"]
```

```python
from contextlib import ExitStack, contextmanager

import concourse.bass as bass
import numpy as np
from concourse import mybir

F32 = mybir.dt.float32
F32R = mybir.dt.float32r
I32 = mybir.dt.int32
ALU = mybir.AluOpType
ACT = mybir.ActivationFunctionType
AX_X = mybir.AxisListType.X
ds = bass.ds

P = 128
SEQ = 512
NT = SEQ // P
DM = 1024
KT = DM // P
DFF = 2816
FT = DFF // P
HEADS = 16
DI = 2048
IT = DI // P
SSD_GROUPS = 8
HPG = 4
SSD_HEADS = 32
GLA_HEADS = 4
GC = 64
NGC = SEQ // GC
RANK = 16
EPS = 1e-6
NEG = -1e30
NBUCKETS = 32
START_AT_ONE = """cu_done c_ready a_done0 a_done1 sil_ready0 sil_ready1 pt_ready o_done pv prob_turned
y_bank_free skip_ready sz_squared
sz_ready go_free gs_ready gz_used gz_ready""".split()
S_ORDER = (0, 2, 1, 3)
UNIT = 2048
HALF_FFN = FT // 2

VEC_ROWS = [("mix_norm", 16), ("ffn_norm", 16), ("final_norm", 8), ("conv_kernel", 24), ("ssd_norm_2", 8),
            ("ssd_gnorm_2", 16), ("gla_norm_2", 8), ("gla_b_gate_2", 8), ("gla_onorm_2", 4), ("final_norm_2", 8)]
VEC = {}
_at = 0
for _name, _rows in VEC_ROWS:
    VEC[_name] = _at
    _at += _rows
NVEC = _at
TAP = 128

INPUTS = ["x", "mix_norm", "ffn_norm", "final_norm", "conv_w_in", "conv_kernel", "conv_w_out", "attn_w_qkv", "attn_w_out",
          "rel_bias", "ffn_w_gate", "ffn_w_up", "ffn_w_down", "ssd_norm_2", "ssd_w_in_2", "ssd_conv_w_2", "ssd_conv_b_2",
          "ssd_dt_bias_2", "ssd_a_log_2", "ssd_d_2", "ssd_gnorm_2", "ssd_w_out_2", "gla_norm_2", "gla_w_in_2",
          "gla_w_gate_2", "gla_b_gate_2", "gla_onorm_2", "gla_w_out_2", "final_norm_2"]

U_CONV_CU, U_CONV_B, U_CONV_OUT = 0, 8, 12
U_FFN0, U_DOWN0 = 16, 38
U_QKV, U_ATTN_OUT = 54, 66
U_FFN1, U_DOWN1 = 70, 92
U_XBC, U_SZ, U_SSD_OUT = 108, 124, 132
U_GQK, U_GV, U_GZ, U_GLA_OUT = 140, 144, 152, 160
U_END = 168

STAGES = ["conv", "ffn0", "attn", "ffn1", "mid", "ssd", "gla", "end"]


def bucket_rows():
    d = 511 - np.arange(640)
    df = np.maximum(d, 1).astype(np.float32)
    exact = NBUCKETS // 2
    large = exact + (np.log(df / np.float32(exact)) / np.float32(np.log(2048 / exact)) * (NBUCKETS - exact)).astype(np.int32)
    bucket = np.where(d < exact, d, np.minimum(large, NBUCKETS - 1))
    rows = np.zeros((NBUCKETS + 1, 640), np.float32)
    for b in range(NBUCKETS):
        rows[b] = (bucket == b) & (d >= 0)
    times = (d <= 128).astype(int) + (d % 4 == 0) + (d % 16 == 0)
    rows[NBUCKETS] = np.where((d >= 0) & (times > 0), np.log(np.maximum(times, 1)), NEG)
    return rows


class Chain:

    def __init__(self, eng, sem):
        self.eng, self.sem, self.n, self.extra = eng, sem, 0, 0

    def __call__(self, ins):
        ins.then_inc(self.sem, 1)
        self.n += 1
        self.eng.wait_ge(self.sem, self.n + self.extra)

    def note(self, ins):
        ins.then_inc(self.sem, 1)
        self.n += 1

    @contextmanager
    def loop(self, count, per, start=0):
        n0, extra0 = self.n, self.extra
        with self.eng.Fori(start, start + count) as i:
            self.extra = extra0 + per * (i - start)
            yield i
            assert self.n - n0 == per, (self.n - n0, per)
        self.n, self.extra = n0 + per * count, extra0


def build(nc, A, out, stop=None):
    stages = STAGES[:STAGES.index(stop) + 1] if stop else STAGES
    on = lambda name: name in stages
    ends = {"conv": U_FFN0, "ffn0": U_QKV, "attn": U_FFN1, "ffn1": U_XBC, "mid": U_XBC, "ssd": U_GQK, "gla": U_END, "end": U_END}
    u_end = ends[stages[-1]]
    toeplitz = nc.dram_tensor("toeplitz", (HEADS, 640), F32, kind="Internal").ap()

    with ExitStack() as ctx:
        def sb(name, shape, dt=F32, c=ctx):
            return c.enter_context(nc.sbuf_tensor(name, shape, dt))

        sems = {}

        def S(name):
            if name not in sems:
                sems[name] = ctx.enter_context(nc.semaphore(name))
            return sems[name]

        bank = [ctx.enter_context(nc.psum_tensor(f"bank{i}", [P, 512], F32)) for i in range(8)]

        xT = sb("xT", [P, KT * SEQ])
        raw = [sb(f"raw{i}", [P, UNIT]) for i in range(2)]
        whi = [sb(f"whi{i}", [P, UNIT], F32R) for i in range(2)]
        wlo = [sb(f"wlo{i}", [P, UNIT], F32R) for i in range(2)]
        hHi = sb("hHi", [P, KT * SEQ], F32R)
        hLo = sb("hLo", [P, KT * SEQ], F32R)
        ident = sb("ident", [P, P])
        ones = sb("ones", [P, P])
        LE = sb("LE", [P, P])
        GE = sb("GE", [P, P])
        GT = sb("GT", [P, P])
        LT = sb("LT", [P, P])
        vecT = sb("vecT", [P, TAP + 192])
        rstd = sb("rstd", [P, SEQ])
        stat = sb("stat", [P, 64])
        t32 = [sb(f"t32_{i}", [P, SEQ]) for i in range(2)]

        @contextmanager
        def scope(spec):
            with ExitStack() as c:
                yield {n: sb(n, s, d, c) for n, s, d in spec}

        def area(spec):
            with scope(spec) as m:
                return m

        R8, V = [P, KT * SEQ], [P, SEQ]
        m_in = area([("xtok", R8, F32), ("vrows", [P, 3 * P], F32)])
        m_conv = area([("cu", [P, KT * 514], F32), ("c0", V, F32), ("c1", V, F32), ("cacc", [P, 2 * SEQ], F32),
                       ("yHi", R8, F32R), ("yLo", R8, F32R)])
        m_ffn = [area([(f"f{j}aHi", [P, FT * SEQ], F32R), (f"f{j}aLo", [P, FT * SEQ], F32R),
                       (f"f{j}sil", [P, 2 * SEQ], F32)]) for j in range(2)]
        m_att = area([("qk", [P, 2 * KT * SEQ], F32), ("vtok", R8, F32), ("otok", R8, F32), ("qF", V, F32), ("qS", V, F32), ("kS", V, F32),
                      ("prob0", [P, 1280], F32), ("prob1", [P, 1280], F32), ("pT", [P, 1280], F32), ("G0", V, F32), ("G1", V, F32),
                      ("rb", [NBUCKETS + 1, HEADS], F32), ("bkt", [NBUCKETS + 1, 640], F32),
                      ("toe", [HEADS, 640], F32), ("ast", [P, 32], F32)])
        with scope([("sY", [P, NT * DI], F32)]) as m_y:
            m_ssd = area([("wdtHi", [P, KT * 64], F32R), ("wdtLo", [P, KT * 64], F32R),
                          ("dtb", [P, 64], F32), ("alog", [P, 64], F32), ("dsk", [P, 32], F32),
                          ("dt", [P, 256], F32), ("dtA", [P, 256], F32), ("la", [P, 256], F32),
                          ("ecum", [P, 256], F32), ("etot", [P, 256], F32), ("wst", [P, 256], F32),
                          ("xpad", [P, 4 * 516], F32), ("xc", [P, 4 * SEQ], F32), ("xt", [P, NT * 256], F32),
                          ("bt", [P, SEQ], F32), ("CB", [P, 2 * SEQ], F32), ("Rm", [P, 2 * SEQ], F32),
                          ("MT", [P, 4 * SEQ], F32), ("xdt", [P, 4 * 256], F32), ("xw", [P, 2 * 256], F32),
                          ("stt", [P, 2 * NT * 256], F32), ("yt", [P, 2 * 256], F32), ("xd", [P, 256], F32)])
            m_ssd2 = area([("szs", [P, 2 * SEQ], F32), ("sHi", R8, F32R), ("sLo", R8, F32R)])
            m_ssd.update(m_y)
        with scope([("gO", [P, NT * DI], F32)]) as m_o:
            with scope([("gQK", [P, 8 * SEQ], F32), ("lg", [P, 2 * SEQ], F32),
                        ("wgf", [2 * RANK, 1024 + P], F32), ("wgs", [2 * RANK, 2 * P], F32), ("m64", [P, SEQ], F32),
                        ("mF", [P, P], F32), ("mB", [P, P], F32),
                        ("qg", [P, 2 * SEQ], F32), ("kg", [P, 2 * SEQ], F32), ("diff", [P, 2 * SEQ], F32),
                        ("gdec", [P, 2 * NGC], F32), ("attF", [P, P], F32), ("attB", [P, P], F32),
                        ("gst", [P, 7 * SEQ], F32), ("gsb", [P, 2 * SEQ], F32)]) as m_gla:
                m_gla.update(area([("gv", [P, NT * SEQ], F32)]))
                m_gl = area([("wglHi", [P, KT * 32], F32R), ("wglLo", [P, KT * 32], F32R), ("gl", [P, NT * 32], F32)])
            m_gla2 = area([("gzs", [P, 2 * SEQ], F32), ("gHi", R8, F32R), ("gLo", R8, F32R)])
            m_gla.update(m_o)
        m_end = area([("otk", R8, F32)])

        def tile(t, k, n=SEQ):
            return t[:, ds(k * n, n)]

        def col(name, k=0):
            return vecT[:, ds(VEC[name] + k, 1)]

        def tapcol(tap, k):
            return vecT[:, ds(TAP + 32 * tap + k, 1)]

        def v3(ap, a):
            return ap.rearrange("p (a b) -> p a b", a=a)

        def bc(ap, n):
            return ap.unsqueeze(2).broadcast_to([ap.shape[0], ap.shape[1], n])

        def rep(ap, n):
            return ap.unsqueeze(1).broadcast_to([ap.shape[0], n, ap.shape[1]])

        def heads(name, c, d, g):
            return m_ssd[name][:, ds(64 * c + 32 * d + HPG * g, HPG)]

        def h4(ap):
            return ap.rearrange("p (h e) -> p h e", h=HPG)

        def inner(k, second, first):
            return tile(first, k) if k < KT else tile(second, k - KT)

        def xw_buf(step, d):
            return t32[step][:, 256 * d:256 * d + 256] if step < 2 else m_ssd["xw"][:, 256 * d:256 * d + 256]

        def ssd_chunk(step, d):
            return step if d == 0 else 3 - step

        raw_full = [S("raw_full0"), S("raw_full1")]
        w_hi, w_lo = S("w_hi"), S("w_lo")
        mm = S("mm")
        res_done = S("res_done")
        h_ready = S("h_ready")
        R_IN, R_CONV, R_FFN0, R_ATT, R_FFN1, R_MID, R_SSD, R_GLA = range(8)
        last_r = {"conv": 1, "ffn0": 2, "attn": 3, "ffn1": 4, "mid": 5, "ssd": 6, "gla": 7, "end": 7}[stages[-1]]

        block = ctx.enter_context(nc.Block())

        @block.sync
        def _(sp):
            sp.dma_start(v3(m_in["xtok"][:, :], NT), A["x"][0].rearrange("(t p) c -> p t c", p=P)).then_inc(S("x_in"), 16)
            for name, rows in VEC_ROWS:
                flat = A[name]
                flat = flat.rearrange({1: "(r p) -> r p", 2: "a (r p) -> (a r) p", 3: "a b (r p) -> (a b r) p"}[len(flat.shape)], p=P)
                sp.dma_start(m_in["vrows"][VEC[name]:VEC[name] + rows, 0:P], flat).then_inc(S("vec_in"), 16)
            taps = A["ssd_conv_w_2"][0].rearrange("a (r p) -> (a r) p", p=P)
            sp.dma_start(m_in["vrows"][:, P:2 * P], taps[0:P]).then_inc(S("vec_in"), 16)
            sp.dma_start(m_in["vrows"][0:32, 2 * P:3 * P], taps[P:160]).then_inc(S("vec_in"), 16)
            sp.dma_start(m_in["vrows"][32:64, 2 * P:3 * P], A["ssd_conv_b_2"].rearrange("a (r p) -> (a r) p", p=P)).then_inc(S("vec_in"), 16)

            def load(n, s, src):
                if not isinstance(n, int) or n >= 2:
                    sp.wait_ge(w_lo, n - 1)
                if isinstance(src, tuple):
                    dst = v3(raw[s][:, :], KT)
                    pieces = [(dst[:, :, P * e:P * (e + 1)], src[e]) for e in range(2)]
                else:
                    kt, w = src.shape[1:]
                    dst = v3(raw[s][:, 0:kt * w], kt)
                    cut = (kt + 1) // 2
                    pieces = [(dst[:, 0:cut, :], src[:, 0:cut, :]), (dst[:, cut:kt, :], src[:, cut:kt, :])]
                for to, frm in pieces:
                    sp.dma_start(to, frm).then_inc(raw_full[s], 16)

            def cols(W, at, n=256):
                return W.rearrange("(k p) n -> p k n", p=P)[:, :, ds(at, n)]

            def pairs(u0, n_pairs, src):
                with sp.Fori(0, n_pairs) as i:
                    for s in range(2):
                        load(u0 + 2 * i + s, s, src(i, s))

            W = A["conv_w_in"][0]
            for s in range(2):
                load(s, s, cols(W, (1 + s) * DM))
            for name in START_AT_ONE:
                sp.sem_inc(S(name), 1)
            with sp.Fori(1, 4) as i:
                for s in range(2):
                    load(2 * i + s, s, cols(W, (1 + s) * DM + 256 * i))
            pairs(U_CONV_B, 2, lambda i, s: cols(W, 512 * i + 256 * s))
            pairs(U_CONV_OUT, 2, lambda i, s: cols(A["conv_w_out"][0], 512 * i + 256 * s))

            def ffn(j, u_up, u_down):
                pairs(u_up, FT // 2, lambda i, s: cols(A[("ffn_w_gate", "ffn_w_up")[s]][j], 256 * i))
                down = A["ffn_w_down"][j]
                pairs(u_down, KT, lambda i, s: cols(down[HALF_FFN * P * s:HALF_FFN * P * (s + 1)], P * i, P))

            if on("ffn0"):
                ffn(0, U_FFN0, U_DOWN0)
            if on("attn"):
                pairs(U_QKV, 6, lambda i, s: cols(A["attn_w_qkv"][0], 512 * i + 256 * s))
                pairs(U_ATTN_OUT, 1, lambda i, s: cols(A["attn_w_out"][0], 512 * i + 256 * s))
                sp.wait_ge(S("toe_ready"), 1)
                sp.dma_start(toeplitz, m_att["toe"][:, :]).then_inc(S("toe_out"), 16)
                sp.wait_ge(S("toe_out"), 16)

                def bias_tile(pr, hh):
                    src = bass.AP(tensor=toeplitz.tensor, offset=640 * (2 * pr + hh), ap=[[1, P], [1, SEQ]])
                    sp.dma_start(m_att[f"G{hh}"][:, :], src).then_inc(S(f"g_in{hh}"), 16)

                for hh in range(2):
                    bias_tile(0, hh)
                with sp.Fori(1, HEADS // 2) as pr:
                    for hh in range(2):
                        sp.wait_ge(S("scored"), 4 * (2 * pr + hh - 1))
                        bias_tile(pr, hh)
                pairs(U_ATTN_OUT + 2, 1, lambda i, s: cols(A["attn_w_out"][0], 512 * (i + 1) + 256 * s))
            if on("ffn1"):
                ffn(1, U_FFN1, U_DOWN1)
            if on("ssd"):
                W = A["ssd_w_in_2"][0]
                pairs(U_XBC, 8, lambda i, s: tuple(cols(W, 2 * DI + DM * e + P * i, P) for e in range(2)) if s else cols(W, DI + 256 * i))
                pairs(U_SZ, 4, lambda i, s: cols(W, 512 * i + 256 * s))
                pairs(U_SSD_OUT, 4, lambda i, s: cols(A["ssd_w_out_2"][0], 256 * i + P * s, P))
            if on("gla"):
                W = A["gla_w_in_2"][0]
                pairs(U_GQK, 2, lambda i, s: tuple(cols(W, 512 * e + 256 * i + P * s, P) for e in range(2)))
                pairs(U_GV, 4, lambda i, s: cols(W, 1024 + 512 * i + 256 * s))
                pairs(U_GZ, 4, lambda i, s: cols(W, 1024 + DI + 512 * i + 256 * s))
                pairs(U_GLA_OUT, 4, lambda i, s: cols(A["gla_w_out_2"][0], 256 * i + P * s, P))
            for t in range(NT):
                sp.wait_ge(S("out_ready"), 8 * (t + 1))
                sp.dma_start(out[0, P * t:P * (t + 1), :], m_end["otk"][:, DM * t:DM * (t + 1)]).then_inc(S("out_done"), 16)
            sp.wait_ge(S("out_done"), 16 * NT)

        @block.gpsimd
        def _(pool):
            n = 0
            cst = S("cst")

            def step(ins):
                nonlocal n
                ins.then_inc(cst, 1)
                n += 1

            step(pool.memset(ident[:, :], 0.0))
            for m in (ones, LE, GE, GT, LT):
                step(pool.memset(m[:, :], 1.0))
            pool.wait_ge(cst, n)
            step(pool.affine_select(out=ident[:, :], in_=ident[:, :], compare_op=ALU.not_equal, fill=1.0, base=0,
                                    pattern=[[1, P]], channel_multiplier=-1))
            for m, op, sign in ((LE, ALU.is_ge, 1), (GE, ALU.is_ge, -1), (GT, ALU.is_gt, -1), (LT, ALU.is_gt, 1)):
                step(pool.affine_select(out=m[:, :], in_=m[:, :], compare_op=op, fill=0.0, base=0,
                                        pattern=[[sign, P]], channel_multiplier=-sign))
            assert n == 11

            def low(k, s):
                pool.wait_ge(w_hi, k)
                pool.tensor_tensor(wlo[s][:, :], raw[s][:, :], whi[s][:, :].bitcast(F32), ALU.subtract).then_inc(w_lo, 1)

            def lows(u0, u1):
                with pool.Fori(u0 // 2, u1 // 2) as i:
                    for s in range(2):
                        low(2 * i + s + 1, s)

            def ssd_group(g, split):
                m = m_ssd
                pool.wait_ge(S("xt_ready"), 3 * g + 2)
                for step in range(3):
                    for d in range(2):
                        c = ssd_chunk(step, d)
                        pool.tensor_tensor(h4(xw_buf(step, d)), h4(m["xt"][:, 256 * c:256 * c + 256]), bc(heads("wst", c, d, g), 64),
                                           ALU.mult).then_inc(S("xw_ready"), 1)
                for c in range(NT):
                    for d, mask in enumerate((LE, GE)):
                        if c:
                            pool.wait_ge(S("seg"), 8 * g + 2 * (c - 1) + d + 1)
                        pool.tensor_tensor(v3(m["Rm"][:, SEQ * d:SEQ * (d + 1)], HPG), bc(heads("la", c, d, g), P), rep(mask[:, :], HPG),
                                           ALU.mult).then_inc(S("rm_ready"), 1)
                    if c >= 2:
                        pool.wait_ge(S("y_mm"), 4 * g + c - 1)
                    for d in range(2):
                        at = 512 * (c % 2) + 256 * d
                        pool.tensor_tensor(h4(m["xdt"][:, at:at + 256]), h4(m["xt"][:, 256 * c:256 * c + 256]), bc(heads("dt", c, d, g), 64),
                                           ALU.mult).then_inc(S("xdt_ready"), 1)
                    if c == 2 and split:
                        low(U_XBC + 2 * g + 4 + 1, 0)
                if split == 2:
                    low(U_XBC + 2 * g + 5 + 1, 1)

            if on("ssd"):
                lows(0, U_XBC + 4)
                pool.wait_ge(S("la_ready"), 1)
                pool.wait_ge(S("wst_ready"), 1)
                with pool.Fori(0, SSD_GROUPS - 2) as g:
                    ssd_group(g, 2)
                ssd_group(SSD_GROUPS - 2, 1)
                ssd_group(SSD_GROUPS - 1, 0)
                low(U_SZ + 1 + 1, 1)
                lows(U_SZ + 2, u_end)
            else:
                lows(0, u_end)

        @block.scalar
        def _(act):
            chain = Chain(act, S("act_chain"))

            def high(n, s, k=None):
                act.wait_ge(raw_full[s], 32 * (n // 2 + 1 if k is None else k))
                if not isinstance(n, int) or n >= 2:
                    act.wait_ge(mm, 2 * (n - 1))
                act.activation(whi[s][:, :], raw[s][:, :], ACT.Copy).then_inc(w_hi, 1)

            def ahead(u0, i, s, per=2):
                if isinstance(i, int) and u0 + per * i + s + 1 >= u_end:
                    return
                high(u0 + per * i + s + 1, (s + 1) % 2, u0 // 2 + (per // 2) * i + (s + 1) // 2 + 1)

            def loop(u0, count, per=2, steps=0):
                if u0 + per * count < u_end:
                    with chain.loop(count, steps) as i:
                        yield i
                else:
                    if count > 1:
                        with chain.loop(count - 1, steps) as i:
                            yield i
                    yield count - 1

            def copy(dst, src, sem, scale=1.0):
                act.activation(dst, src, ACT.Copy, scale=scale).then_inc(sem, 1)

            def norm(j):
                for k in range(KT):
                    act.wait_ge(res_done, 8 * j + k + 1)
                    if 8 * j + k >= 2:
                        act.wait_ge(S("sq_used"), 8 * j + k - 1)
                    act.activation(t32[k % 2][:, :], tile(xT, k), ACT.Square).then_inc(S("sq_ready"), 1)
                act.wait_ge(S("mean_ready"), j + 1)
                act.activation(rstd[:, :], rstd[:, :], ACT.Sqrt).then_inc(S("root_ready"), 1)
                if j not in (4, 7):
                    for k in range(KT):
                        n = 8 * (j - (j > 4)) + k + 1
                        act.wait_ge(S("normed"), n)
                        copy(tile(hHi, k), t32[k % 2][:, :], S("h_hi"))

            def turned_high(name, hi, vec, vec_tiles):
                for k in range(IT):
                    act.wait_ge(S(name + "_turned"), k + 1)
                    act.activation(hi(k), bank[k % 4][:, :], ACT.Copy, scale=col(vec, k % vec_tiles)).then_inc(S(name + "_hi"), 1)

            high(0, 0)
            act.wait_ge(S("vec_turned"), 3)
            copy(vecT[:, 0:NVEC], bank[4][:, 0:NVEC], S("vec_ready"))
            copy(vecT[:, TAP:TAP + 192], bank[4][:, TAP:TAP + 192], S("vec_ready"))

            norm(0)
            for i in loop(0, 4):
                for s in range(2):
                    ahead(0, i, s)
                    if s == 0:
                        for b in range(2):
                            act.wait_ge(mm, 4 * i + b + 1)
                            act.wait_ge(S("cu_done"), 2 * i + 1)
                            copy(m_conv[f"c{b}"][:, :], bank[b][:, :], S("c_ready"))
            for i in loop(U_CONV_B, 2):
                for s in range(2):
                    ahead(U_CONV_B, i, s)
            for i in loop(U_CONV_OUT, 2):
                for s in range(2):
                    ahead(U_CONV_OUT, i, s)

            def ffn(j, u_up, u_down):
                norm(2 * j + 1)
                for i in loop(u_up, FT // 2):
                    for s in range(2):
                        ahead(u_up, i, s)
                        if s == 0:
                            for b in range(2):
                                act.wait_ge(mm, 2 * u_up + 4 * i + b + 1)
                                act.wait_ge(S(f"a_done{j}"), 2 * i + 1)
                                act.activation(tile(m_ffn[j][f"f{j}sil"], b), bank[b][:, :], ACT.Silu).then_inc(S(f"sil_ready{j}"), 1)
                for i in loop(u_down, KT):
                    for s in range(2):
                        ahead(u_down, i, s)

            if on("ffn0"):
                ffn(0, U_FFN0, U_DOWN0)

            if on("attn"):
                act.wait_ge(res_done, 8 * (R_FFN0 + 1))
                act.dma_start(m_att["rb"][0:NBUCKETS, :], A["rel_bias"]).then_inc(S("bias_in"), 16)
                act.dma_start(m_att["bkt"][:, :], A["bucket_rows"]).then_inc(S("bias_in"), 16)
                act.wait_ge(S("toe_mm"), 2)
                copy(m_att["toe"][:, 0:SEQ], bank[5][0:HEADS, :], S("act_toe"))
                act.activation(m_att["toe"][:, SEQ:640], bank[6][0:HEADS, 0:P], ACT.Copy).then_inc(S("toe_half"), 1)
                act.wait_ge(S("act_toe"), 1)
                act.wait_ge(S("toe_half"), 1)
                act.sem_inc(S("toe_ready"), 1)
                norm(2)
                qk = m_att["qk"]
                act.sem_inc(S("qkv_free"), 4)
                for i in loop(U_QKV, 4):
                    for s in range(2):
                        ahead(U_QKV, i, s)
                        for b in range(2):
                            act.wait_ge(mm, 2 * U_QKV + 4 * i + 2 * s + b + 1)
                            copy(tile(qk, 4 * i + 2 * s + b), bank[2 * s + b][:, :], S("qkv_free"))
                vt = v3(m_att["vtok"][:, :], NT)
                for i in loop(U_QKV + 8, 2):
                    for s in range(2):
                        ahead(U_QKV + 8, i, s)
                        for hf in range(2):
                            act.wait_ge(mm, 2 * (U_QKV + 8) + 4 * i + 2 * s + hf + 1)
                            copy(vt[:, 2 * hf:2 * hf + 2, ds(512 * i + 256 * s, 256)], v3(bank[2 * s + hf][:, :], 2), S("qkv_free"))
                ast = m_att["ast"]

                def stage_q(pr):
                    act.wait_ge(S("scores"), 8 * pr)
                    copy(m_att["qF"][:, :], tile(qk, pr), S("qf_ready"), scale=64 ** -0.5)
                    copy(m_att["kS"][:, :], tile(qk, KT + pr), S("qs_ready"))
                    act.wait_ge(S("qf_ready"), pr + 1)
                    copy(v3(m_att["qS"][:, :], NT), v3(m_att["qF"][:, :], NT)[:, :, ::-1], S("qs_ready"))

                def exponentials(pr, hh):
                    prob = m_att[f"prob{hh}"]
                    act.wait_ge(S("scored"), 4 * (2 * pr + hh) + 4)
                    for i in S_ORDER:
                        reg = slice(64 * i * (i + 1), 64 * (i + 1) * (i + 2))
                        act.activation(prob[:, reg], prob[:, reg], ACT.Exp, bias=ast[:, 16 * hh + 4 + i:16 * hh + 5 + i],
                                       accum_out=ast[:, 16 * hh + 8 + i:16 * hh + 9 + i]).then_inc(S("prob_ready"), 1)

                def turned(pr, hh):
                    hd, pT = 2 * pr + hh, m_att["pT"]
                    act.wait_ge(S("pv"), hd + 1)
                    for j in range(NT):
                        act.wait_ge(S("prob_turned"), 4 * hd + j + 1 + 1)
                        w = P * (NT - j)
                        at = [0, 512, 896, 1152][j]
                        copy(pT[:, at:at + w], bank[j][:, 0:w], S("pt_ready"))

                act.wait_ge(S("qkv_free"), 4 + 16 + 8)
                LAST = HEADS // 2 - 1

                def head_pair(pr):
                    exponentials(pr, 1)
                    turned(pr, 0)
                    exponentials(pr + 1, 0)
                    turned(pr, 1)

                stage_q(0)
                stage_q(1)
                exponentials(0, 0)
                with act.Fori(0, LAST - 1) as pr:
                    head_pair(pr)
                    stage_q(pr + 2)
                head_pair(LAST - 1)
                exponentials(LAST, 1)
                turned(LAST, 0)
                turned(LAST, 1)
                for i in loop(U_ATTN_OUT, 2):
                    for s in range(2):
                        ahead(U_ATTN_OUT, i, s)

            if on("ffn1"):
                ffn(1, U_FFN1, U_DOWN1)
            if on("mid"):
                norm(4)

            if on("ssd"):
                m = m_ssd
                act.wait_ge(S("mid_done"), 8)
                act.dma_start(v3(m_ssd["Rm"][:, 0:SEQ], KT), A["ssd_w_in_2"][0, :, DI + 4096:DI + 4096 + 64].rearrange("(k p) n -> p k n", p=P)).then_inc(S("ssd_in"), 16)
                for name, src in (("dtb", "ssd_dt_bias_2"), ("alog", "ssd_a_log_2")):
                    row = A[src].rearrange("a d h -> a (d h)")
                    act.dma_start(m_ssd[name][:, :], row.broadcast_to([P, 64])).then_inc(S("ssd_in"), 16)
                act.dma_start(m_ssd["dsk"][:, :], A["ssd_d_2"].broadcast_to([P, 32])).then_inc(S("ssd_in"), 16)
                act.wait_ge(S("ssd_in"), 64)
                act.activation(m["alog"][:, :], m["alog"][:, :], ACT.Exp).then_inc(S("a_exp"), 1)
                norm(5)
                high(U_XBC + 1, 1)
                act.wait_ge(S("dt_pre"), 1)
                chain(act.activation(m["dtA"][:, :], m["dt"][:, :], ACT.Abs))
                chain(act.activation(m["dtA"][:, :], m["dtA"][:, :], ACT.Exp, scale=-1.0))
                act.activation(m["dtA"][:, :], m["dtA"][:, :], ACT.Ln, bias=1.0).then_inc(S("dt_log"), 1)

                def to_xpad(g, q):
                    act.wait_ge(mm, 2 * U_XBC + 4 * g + q + 1)
                    copy(m["xpad"][:, 516 * q + 2:516 * q + 514], bank[q][:, :], S("xpad_ready"))

                def silus(g):
                    for q in range(4):
                        ct = 2 * g + q if q < 2 else (16 if q == 2 else 24) + g
                        act.wait_ge(S("tap_done"), 4 * g + q + 1)
                        act.activation(tile(m["xc"], q), tile(m["xc"], q), ACT.Silu, bias=tapcol(5, ct)).then_inc(S("xc_ready"), 1)

                def group(g, more, split):
                    act.wait_ge(S("skip_ready"), 4 * g + 1)
                    for b in range(3):
                        act.wait_ge(S("x_turned"), 3 * g + b + 1)
                        dst = m["bt"][:, :] if b == 2 else m["xt"][:, 512 * b:512 * b + 512]
                        copy(dst, bank[4 + b][:, :], S("xt_ready"))
                    if more:
                        to_xpad(g + 1, 0)
                    for c in range(NT):
                        for d in range(2):
                            act.wait_ge(S("seg"), 8 * g + 2 * c + d + 1)
                            act.activation(tile(m["MT"], 2 * (c % 2) + d), bank[4 + d][:, :], ACT.Exp).then_inc(S("ex_ready"), 1)
                        if more and c < 3:
                            to_xpad(g + 1, c + 1)
                        if split and c == 1:
                            high(U_XBC + 2 * g + 4, 0, U_XBC // 2 + g + 3)
                    if more:
                        silus(g + 1)
                    if split == 2:
                        high(U_XBC + 2 * g + 5, 1, U_XBC // 2 + g + 3)

                for q in range(4):
                    to_xpad(0, q)
                    if q % 2:
                        high(U_XBC + 2 + q // 2, q // 2)
                act.wait_ge(S("decays"), 1)
                for b, name in ((5, "ecum"), (6, "wst"), (7, "etot")):
                    act.activation(m[name][:, :], bank[b][:, 0:256], ACT.Exp).then_inc(S("decay_exp"), 1)
                silus(0)
                with act.Fori(0, SSD_GROUPS - 2) as g:
                    group(g, True, 2)
                group(SSD_GROUPS - 2, True, 1)
                group(SSD_GROUPS - 1, False, 0)
                for i in loop(U_SZ, 4):
                    for s in range(2):
                        ahead(U_SZ, i, s)
                        for hf in range(2):
                            act.wait_ge(mm, 2 * U_SZ + 4 * i + 2 * s + hf + 1)
                            zs = tile(m_ssd2["szs"], hf)
                            act.wait_ge(S("sz_squared"), 8 * i + 4 * s + 1)
                            act.activation(zs, bank[2 * s + hf][:, :], ACT.Silu).then_inc(S("sz_ready"), 1)
                            act.wait_ge(S("sz_used"), 4 * i + 2 * s + hf + 1)
                            for e in range(2):
                                act.activation(zs[:, 256 * e:256 * e + 256],
                                               v3(m_ssd["sY"][:, :], NT)[:, 2 * hf + e, ds(512 * i + 256 * s, 256)], ACT.Square,
                                               accum_out=stat[:, ds(8 * (2 * hf + e) + 2 * i + s, 1)]).then_inc(S("sz_squared"), 1)
                act.wait_ge(S("ssq_mean"), 1)
                act.activation(stat[:, 0:32], stat[:, 0:32], ACT.Sqrt).then_inc(S("ssq_root"), 1)
                turned_high("sy", lambda k: inner(k, m_ssd2["sHi"], hHi), "ssd_gnorm_2", IT)
                for i in loop(U_SSD_OUT, 4):
                    for s in range(2):
                        ahead(U_SSD_OUT, i, s)

            if on("gla"):
                m = m_gla
                act.wait_ge(res_done, 8 * (R_SSD + 1))
                act.dma_start(v3(m_gla["kg"][:, 0:256], KT), A["gla_w_in_2"][0, :, 1024 + 2 * DI:1024 + 2 * DI + 32].rearrange("(k p) n -> p k n", p=P)).then_inc(S("gla_in"), 16)
                act.wait_ge(S("wgf_zero"), 1)
                for d in range(2):
                    act.dma_start(m_gla["wgf"][RANK * d:RANK * (d + 1), 512 * d:512 * (d + 1)],
                                 A["gla_w_gate_2"][0, d]).then_inc(S("gla_in"), 16)
                norm(6)
                act.sem_inc(S("gqk_free"), 4)
                for i in loop(U_GQK, 2):
                    for s in range(2):
                        ahead(U_GQK, i, s)
                        for b in range(2):
                            act.wait_ge(mm, 2 * U_GQK + 4 * i + 2 * s + b + 1)
                            copy(tile(m["gQK"], 4 * i + 2 * s + b), bank[2 * s + b][:, :], S("gqk_free"), scale=1.0 if b else P ** -0.5)
                act.wait_ge(S("gl_mm"), 1)
                copy(m_gl["gl"][:, :], bank[4][:, 0:128], S("gl_ready"))
                act.wait_ge(S("gl_turned"), 1)
                act.activation(rstd[0:32, :], bank[5][0:32, :], ACT.Copy).then_inc(S("glT_ready"), 1)
                act.wait_ge(S("gla_in"), 48)
                gv = v3(m["gv"][:, :], NT)

                def gate_weights(hd):
                    for d in range(2):
                        act.activation(m["wgs"][:, P * d:P * (d + 1)], m["wgf"][:, ds(512 * d + P * hd, P)], ACT.Copy).then_inc(S("wgs_ready"), 1)

                def values(hd, s, hf):
                    act.wait_ge(mm, 2 * U_GV + 4 * hd + 2 * s + hf + 1)
                    copy(gv[:, 2 * hf:2 * hf + 2, 256 * s:256 * s + 256], v3(bank[hf][:, :], 2), S("gv_ready"))

                def gate_factors(hd, d):
                    act.wait_ge(S("gcum"), 2 * hd + d + 1)
                    last = v3(tile(m["kg"], d), NGC)[:, :, (GC - 1) * (1 - d):(GC - 1) * (1 - d) + 1]
                    act.activation(m["gdec"][:, NGC * d:NGC * (d + 1)].unsqueeze(2), last, ACT.Exp, scale=1 / 16).then_inc(S("gdec_ready"), 1)
                    for dst, src, sc in (("qg", "kg", 1 / 16), ("kg", "kg", -1 / 16), ("diff", "diff", 1 / 16)):
                        if dst == "kg":
                            act.wait_ge(S("gdec_ready"), 2 * hd + d + 1)
                            act.wait_ge(S("g_exp"), 6 * hd + 3 * d + 1)
                        act.activation(tile(m[dst], d), tile(m[src], d), ACT.Exp, scale=sc).then_inc(S("g_exp"), 1)

                def turned_keys(hd, d):
                    act.wait_ge(S("kd_turned"), 2 * hd + d + 1)
                    copy(t32[d][:, :], bank[6][:, :], S("kdt_ready"))

                gate_weights(0)
                for hd in loop(U_GV, 4, steps=4):
                    for d in range(2):
                        act.wait_ge(S("gate_mm"), 2 * hd + d + 1)
                        chain.note(act.activation(tile(m["lg"], d), bank[4 + d][:, :], ACT.Identity, bias=col("gla_b_gate_2", 4 * d + hd)))
                    act.wait_ge(chain.sem, chain.n + chain.extra)
                    chain(act.activation(m["diff"][:, :], m["lg"][:, :], ACT.Abs))
                    chain(act.activation(m["diff"][:, :], m["diff"][:, :], ACT.Exp, scale=-1.0))
                    act.activation(m["diff"][:, :], m["diff"][:, :], ACT.Ln, bias=1.0).then_inc(S("lg_log"), 1)
                    gate_weights(hd + 1)
                    ahead(U_GV, hd, 0)
                    values(hd, 0, 0)
                    gate_factors(hd, 0)
                    values(hd, 0, 1)
                    gate_factors(hd, 1)
                    ahead(U_GV, hd, 1)
                    turned_keys(hd, 0)
                    values(hd, 1, 0)
                    values(hd, 1, 1)
                    turned_keys(hd, 1)
                    for n in range(NT):
                        t = NT - 1 - n
                        out = bank[0 if n % 2 else 3][:, :]
                        act.wait_ge(S("go_mm"), 4 * hd + n + 1)
                        act.activation(v3(m["gO"][:, :], NT)[:, t, ds(512 * hd, 512)], out, ACT.Copy).then_inc(S("go_copy"), 1)
                        act.wait_ge(S("go_free"), 4 * hd + n + 1)
                        act.activation(tile(m["diff"], 0), out, ACT.Square, accum_out=stat[:, ds(4 * t + hd, 1)]).then_inc(S("go_free"), 1)
                act.wait_ge(S("gsq_mean"), 1)
                act.activation(stat[:, 0:16], stat[:, 0:16], ACT.Sqrt).then_inc(S("gsq_root"), 1)
                for i in loop(U_GZ, 4):
                    for s in range(2):
                        ahead(U_GZ, i, s)
                        for hf in range(2):
                            act.wait_ge(mm, 2 * U_GZ + 4 * i + 2 * s + hf + 1)
                            act.wait_ge(S("gz_used"), 4 * i + 2 * s + hf + 1)
                            act.activation(tile(m_gla2["gzs"], hf), bank[2 * s + hf][:, :], ACT.Silu).then_inc(S("gz_ready"), 1)
                turned_high("gy", lambda k: inner(k, m_gla2["gHi"], hHi), "gla_onorm_2", 4)
                for i in loop(U_GLA_OUT, 4):
                    for s in range(2):
                        ahead(U_GLA_OUT, i, s)

            if on("end"):
                norm(7)
            for t in range(NT):
                for k in range(KT):
                    act.wait_ge(S("out_turned"), KT * t + k + 1)
                    copy(m_end["otk"][:, DM * t + P * k:DM * t + P * (k + 1)], bank[k % 4][:, 0:P], S("out_ready"))

        @block.vector
        def _(dve):
            chain = Chain(dve, S("dve_chain"))
            tt, ts, stt3 = dve.tensor_tensor, dve.tensor_scalar, dve.scalar_tensor_tensor

            def norm(j, name, k0=0, to="h"):
                dve.wait_ge(S("sums"), j + 1)
                ts(rstd[:, :], bank[4][:, :], 1.0 / DM, EPS, ALU.mult, ALU.add).then_inc(S("mean_ready"), 1)
                dve.wait_ge(S("root_ready"), j + 1)
                chain(dve.reciprocal(rstd[:, :], rstd[:, :]))
                n0 = 8 * (j - (j > 4))

                def normed(k):
                    if k >= 2:
                        dve.wait_ge(h_ready, n0 + k - 1)
                    stt3(t32[k % 2][:, :], tile(xT, k), col(name, k0 + k), rstd[:, :], ALU.mult, ALU.mult).then_inc(S("normed"), 1)

                if to == "x":
                    for k in range(KT):
                        stt3(tile(xT, k), tile(xT, k), col(name, k0 + k), rstd[:, :], ALU.mult, ALU.mult).then_inc(res_done, 1)
                    return
                normed(0)
                normed(1)
                for k in range(KT):
                    dve.wait_ge(S("h_hi"), n0 + k + 1)
                    tt(tile(hLo, k), t32[k % 2][:, :], tile(hHi, k).bitcast(F32), ALU.subtract).then_inc(h_ready, 1)
                    if k + 2 < KT:
                        normed(k + 2)

            def residual(r, count, per, mark, n_loop, free):
                dve.sem_inc(S(free), count)
                with dve.Fori(0, n_loop) as i:
                    for q in range(per):
                        dve.wait_ge(mm, mark(i, q))
                        x = tile(xT, per * i + q)
                        tt(x, x, bank[q][:, :], ALU.add).then_inc(res_done, 1)
                        dve.wait_ge(res_done, 8 * r + per * i + q + 1)
                        dve.sem_inc(S(free), 1)

            def turned_low(name, hi, lo, vec, vec_tiles, k):
                dve.wait_ge(S(name + "_hi"), k + 1)
                stt3(lo(k), bank[k % 4][:, :], col(vec, k % vec_tiles), hi(k).bitcast(F32), ALU.mult, ALU.subtract).then_inc(S(name + "_lo"), 1)

            for k in range(KT):
                dve.wait_ge(S("x_turn"), k + 1)
                dve.tensor_copy(tile(xT, k), bank[k % 4][:, :]).then_inc(res_done, 1)
            dve.wait_ge(res_done, 8)
            dve.wait_ge(S("vec_ready"), 2)

            norm(0, "mix_norm")
            cu = m_conv["cu"]
            dve.memset(v3(cu[:, :], KT)[:, :, 0:2], 0.0).then_inc(S("cu_edge"), 1)
            with dve.Fori(0, 4) as i:
                for b in range(2):
                    dve.wait_ge(mm, 4 * i + b + 3)
                    dve.wait_ge(S("c_ready"), 2 * i + b + 1 + 1)
                    tt(cu[:, ds(514 * (2 * i + b) + 2, SEQ)], bank[2 + b][:, :], m_conv[f"c{b}"][:, :], ALU.mult).then_inc(S("cu_done"), 1)
            dve.wait_ge(S("cu_done"), 8 + 1)
            dve.wait_ge(S("cu_edge"), 1)
            dve.sem_inc(S("y_free"), 4)
            with chain.loop(2, 16 + 8) as i:
                for q in range(4):
                    k = 4 * i + q
                    acc = tile(m_conv["cacc"], q % 2)
                    chain(ts(acc, cu[:, ds(514 * k, SEQ)], col("conv_kernel", k), None, ALU.mult))
                    for j in (1, 2):
                        chain(stt3(acc, cu[:, ds(514 * k + j, SEQ)], col("conv_kernel", 8 * j + k), acc, ALU.mult, ALU.add))
                    dve.wait_ge(mm, 2 * U_CONV_B + 4 * i + q + 1)
                    chain(tt(t32[q % 2][:, :], bank[q][:, :], acc, ALU.mult))
                    dve.sem_inc(S("y_free"), 1)
                    chain(dve.tensor_copy(tile(m_conv["yHi"], k), t32[q % 2][:, :]))
                    chain(tt(tile(m_conv["yLo"], k), t32[q % 2][:, :], tile(m_conv["yHi"], k).bitcast(F32), ALU.subtract))
            dve.sem_inc(S("y_ready"), 1)
            residual(R_CONV, 4, 4, lambda i, q: 2 * U_CONV_OUT + 4 * i + q + 1, 2, "conv_free")

            def ffn(j, u_up, u_down):
                norm(2 * j + 1, "ffn_norm", 8 * j)
                f = m_ffn[j]
                aHi, aLo, sil = f[f"f{j}aHi"], f[f"f{j}aLo"], f[f"f{j}sil"]
                with chain.loop(FT // 2, 4) as i:
                    for b in range(2):
                        dve.wait_ge(mm, 2 * u_up + 4 * i + b + 3)
                        dve.wait_ge(S(f"sil_ready{j}"), 2 * i + b + 1 + 1)
                        chain(tt(t32[b][:, :], bank[2 + b][:, :], tile(sil, b), ALU.mult))
                        chain(dve.tensor_copy(tile(aHi, 2 * i + b), t32[b][:, :]))
                        tt(tile(aLo, 2 * i + b), t32[b][:, :], tile(aHi, 2 * i + b).bitcast(F32), ALU.subtract).then_inc(S(f"a_done{j}"), 1)
                residual(2 + 2 * j, 2, 2, lambda i, q: 2 * u_down + 8 * i + 4 * q + 4, 4, f"ffn_free{j}")

            if on("ffn0"):
                ffn(0, U_FFN0, U_DOWN0)

            if on("attn"):
                dve.memset(m_att["rb"][NBUCKETS:NBUCKETS + 1, :], 1.0).then_inc(S("rb_one"), 1)
                norm(2, "mix_norm", 8)
                ast = m_att["ast"]

                def scored(pr, hh):
                    hd = 2 * pr + hh
                    dve.wait_ge(S(f"g_in{hh}"), 16 * (pr + 1))
                    if not isinstance(pr, int):
                        dve.wait_ge(S("prob_turned"), 4 * (hd - 1) + 1)
                    for n, i in enumerate(S_ORDER):
                        w = P * (i + 1)
                        dve.wait_ge(S("scores"), 4 * hd + max(n + 1, 2))
                        dve.sem_inc(S("scores_seen"), 1)
                        src = [bank[4][:, 0:128], bank[5][:, 0:256], bank[4][:, 128:512], bank[6][:, :]][i]
                        reg = slice(64 * i * (i + 1), 64 * (i + 1) * (i + 2))
                        chain.note(dve.tensor_tensor_reduce(m_att[f"prob{hh}"][:, reg], src, m_att[f"G{hh}"][:, SEQ - w:SEQ], 1.0, -3e38,
                                                       ALU.add, ALU.max, ast[:, 16 * hh + i:16 * hh + i + 1]))
                    dve.wait_ge(chain.sem, chain.n + chain.extra)
                    ts(ast[:, 16 * hh + 4:16 * hh + 8], ast[:, 16 * hh:16 * hh + 4], -1.0, None, ALU.mult).then_inc(S("scored"), 4)

                def inverse_sums(pr, hh):
                    hd = 2 * pr + hh
                    dve.wait_ge(S("prob_ready"), 4 * hd + 4)
                    chain(dve.reciprocal(ast[:, 16 * hh + 12:16 * hh + 16], ast[:, 16 * hh + 8:16 * hh + 12]))

                def weighed(pr, hh):
                    hd = 2 * pr + hh
                    dve.wait_ge(S("pv"), hd + 1 + 1)
                    tt(v3(m_att["otok"][:, :], NT)[:, :, ds(64 * hd, 64)], v3(bank[7][:, 0:256], NT),
                       bc(ast[:, 16 * hh + 12:16 * hh + 16], 64), ALU.mult).then_inc(S("o_done"), 1)

                scored(0, 0)
                scored(0, 1)
                with chain.loop(HEADS // 2 - 1, 10) as pr:
                    for hh in range(2):
                        inverse_sums(pr, hh)
                        scored(pr + 1, hh)
                        weighed(pr, hh)
                for hh in range(2):
                    inverse_sums(HEADS // 2 - 1, hh)
                    weighed(HEADS // 2 - 1, hh)
                for k in range(KT):
                    dve.wait_ge(S("o_turned"), k + 1)
                    o = v3(bank[k % 4][:, :], NT)[:, :, ::-1]
                    chain(dve.tensor_copy(v3(tile(hHi, k), NT), o))
                    tt(v3(tile(hLo, k), NT), o, v3(tile(hHi, k).bitcast(F32), NT), ALU.subtract).then_inc(S("ho_ready"), 1)
                residual(R_ATT, 4, 4, lambda i, q: 2 * U_ATTN_OUT + 4 * i + q + 1, 2, "att_free")

            if on("ffn1"):
                ffn(1, U_FFN1, U_DOWN1)
            if on("mid"):
                norm(4, "final_norm", 0, "x")
                dve.wait_ge(res_done, 8 * (R_MID + 1))
                dve.sem_inc(S("mid_done"), 8)

            if on("ssd"):
                m = m_ssd
                dve.wait_ge(S("ssd_in"), 64)
                chain(dve.tensor_copy(m["wdtHi"][:, :], m["Rm"][:, 0:SEQ]))
                tt(m["wdtLo"][:, :], m["Rm"][:, 0:SEQ], m["wdtHi"][:, :].bitcast(F32), ALU.subtract).then_inc(S("wdt_ready"), 1)
                xpad = v3(m["xpad"][:, :], 4)
                dve.memset(xpad[:, :, 0:2], 0.0).then_inc(S("xpad_edge"), 1)
                dve.memset(xpad[:, :, 514:516], 0.0).then_inc(S("xpad_edge"), 1)
                dve.wait_ge(S("xpad_edge"), 2)
                norm(5, "ssd_norm_2")
                dve.wait_ge(S("dt_mm"), 1)
                tt(v3(m["dt"][:, :], NT), v3(bank[4][:, 0:256], NT), rep(m["dtb"][:, :], NT), ALU.add).then_inc(S("dt_pre"), 1)
                dve.wait_ge(S("dt_log"), 1)
                dve.wait_ge(S("dt_pre"), 1)
                chain(stt3(m["dt"][:, :], m["dt"][:, :], 0.0, m["dtA"][:, :], ALU.max, ALU.add))
                dve.wait_ge(S("a_exp"), 1)
                stt3(v3(m["la"][:, :], NT), v3(m["dt"][:, :], NT), -1.0, rep(m["alog"][:, :], NT), ALU.mult, ALU.mult)\
                    .then_inc(S("la_ready"), 1)
                Y = v3(m["sY"][:, :], NT)

                def taps(g, q):
                    ct = 2 * g + q if q < 2 else (16 if q == 2 else 24) + g
                    acc = tile(m["xc"], q)
                    x0 = 516 * q
                    dve.wait_ge(S("xpad_ready"), 4 * g + q + 1)
                    chain(ts(acc, m["xpad"][:, x0:x0 + SEQ], tapcol(0, ct), None, ALU.mult))
                    for j in range(1, 4):
                        chain(stt3(acc, m["xpad"][:, x0 + j:x0 + j + SEQ], tapcol(j, ct), acc, ALU.mult, ALU.add))
                    stt3(acc, m["xpad"][:, x0 + 4:x0 + 4 + SEQ], tapcol(4, ct), acc, ALU.mult, ALU.add).then_inc(S("tap_done"), 1)

                def group(g, more):
                    dve.wait_ge(S("cb_mm"), g + 1)
                    for d, mask in enumerate((LE, GE)):
                        chain.note(tt(v3(tile(m["CB"], d), NT), v3(bank[7][:, :], NT), rep(mask[:, :], NT), ALU.mult))
                    for step in range(3):
                        bufs = []
                        for d in range(2):
                            c = ssd_chunk(step, d)
                            at = 1024 * d + 256 * (c + 1 - 2 * d)
                            bufs.append(m["stt"][:, at:at + 256])
                            if step:
                                chain.note(tt(h4(bufs[d]), h4(m["stt"][:, 1024 * d + 256 * c:1024 * d + 256 * c + 256]),
                                              bc(heads("etot", c, d, g), 64), ALU.mult))
                        for d in range(2):
                            dve.wait_ge(S("state_mm"), 6 * g + 2 * step + d + 1)
                            if step:
                                if d == 0:
                                    dve.wait_ge(chain.sem, chain.n + chain.extra)
                                chain.note(tt(bufs[d], bufs[d], bank[4 + d][:, 0:256], ALU.add))
                            else:
                                chain.note(dve.tensor_copy(bufs[d], bank[4 + d][:, 0:256]))
                        dve.wait_ge(chain.sem, chain.n + chain.extra)
                        dve.sem_inc(S("state_ready"), 1)
                    for c in range(NT):
                        for d in range(2):
                            MT = tile(m["MT"], 2 * (c % 2) + d)
                            dve.wait_ge(S("ex_ready"), 8 * g + 2 * c + d + 1)
                            tt(v3(MT, HPG), v3(MT, HPG), rep(m["CB"][:, SEQ * d + P * c:SEQ * d + P * c + P], HPG),
                               ALU.mult).then_inc(S("mt_ready"), 1)
                        xd, yt = m["xd"][:, :], m["yt"]
                        tt(h4(xd), h4(m["xt"][:, 256 * c:256 * c + 256]), bc(m["dsk"][:, ds(HPG * g, HPG)], 64), ALU.mult)\
                            .then_inc(S("skip_ready"), 1)
                        if more:
                            if c == 3:
                                dve.wait_ge(S("c_read"), g + 1)
                            taps(g + 1, c)
                        dve.wait_ge(S("y_mm"), 4 * g + c + 1)
                        dirs = [d for d in range(2) if not (c == 0 and d == 0) and not (c == 3 and d == 1)]
                        for d in dirs:
                            chain.note(tt(h4(yt[:, 256 * d:256 * d + 256]), h4(bank[7][:, 256 * d:256 * d + 256]), bc(heads("ecum", c, d, g), 64), ALU.mult))
                        dve.wait_ge(S("skip_ready"), 4 * g + c + 1 + 1)
                        chain(tt(xd, xd, bank[6][:, 0:256], ALU.add))
                        dve.sem_inc(S("y_bank_free"), 1)
                        if len(dirs) == 2:
                            chain(tt(xd, xd, yt[:, 0:256], ALU.add))
                        chain(tt(Y[:, c, ds(256 * g, 256)], xd, yt[:, 256 * dirs[-1]:256 * dirs[-1] + 256], ALU.add))

                for q in range(4):
                    taps(0, q)
                dve.wait_ge(S("decay_exp"), 3)
                chain(tt(m["wst"][:, :], m["wst"][:, :], m["dt"][:, :], ALU.mult))
                dve.sem_inc(S("wst_ready"), 1)
                dve.wait_ge(S("la_ready"), 1)

                g_steps = 2 + (2 + 4 + 4) + 4 * 4 + (3 + 5 + 5 + 3)
                with chain.loop(SSD_GROUPS - 1, g_steps) as g:
                    group(g, True)
                group(SSD_GROUPS - 1, False)
                with chain.loop(4, 4) as i:
                    for s in range(2):
                        for hf in range(2):
                            dve.wait_ge(S("sz_ready"), 4 * i + 2 * s + hf + 1 + 1)
                            y = Y[:, 2 * hf:2 * hf + 2, ds(512 * i + 256 * s, 256)]
                            chain(tt(y, y, v3(tile(m_ssd2["szs"], hf), 2), ALU.mult))
                            dve.sem_inc(S("sz_used"), 1)
                dve.wait_ge(S("sz_squared"), 32 + 1)
                ts(stat[:, 0:32], stat[:, 0:32], 1.0 / 256, EPS, ALU.mult, ALU.add).then_inc(S("ssq_mean"), 1)
                dve.wait_ge(S("ssq_root"), 1)
                chain(dve.reciprocal(stat[:, 0:32], stat[:, 0:32]))

                def scaled(g):
                    y = Y[:, :, 256 * g:256 * g + 256]
                    tt(y, y, v3(stat[:, 0:32], NT)[:, :, g:g + 1].broadcast_to([P, NT, 256]), ALU.mult).then_inc(S("sy_scaled"), 1)

                scaled(0)
                scaled(1)
                for k in range(IT):
                    turned_low("sy", lambda k: inner(k, m_ssd2["sHi"], hHi), lambda k: inner(k, m_ssd2["sLo"], hLo), "ssd_gnorm_2", IT, k)
                    if k % 2 and k // 2 + 2 < SSD_GROUPS:
                        scaled(k // 2 + 2)
                residual(R_SSD, 2, 2, lambda i, q: 2 * U_SSD_OUT + 4 * i + 2 * q + 2, 4, "ssd_free")

            if on("gla"):
                m = m_gla
                dve.memset(m["wgf"][:, :], 0.0).then_inc(S("wgf_zero"), 1)
                chain(dve.tensor_copy(m["mF"][:, :], LE[:, :]))
                chain(dve.memset(m["mF"][0:GC, GC:P], 0.0))
                chain(dve.tensor_copy(m["mB"][:, :], GE[:, :]))
                chain(dve.memset(m["mB"][GC:P, 0:GC], 0.0))
                chain(dve.memset(m["attF"][:, :], 0.0))
                chain(dve.memset(m["attB"][:, :], 0.0))
                chain(dve.memset(m["m64"][:, :], 1.0))
                chain(dve.memset(v3(m["m64"][:, :], NGC)[:, :, 0:1], 0.0))
                dve.wait_ge(S("gla_in"), 48)
                chain(dve.tensor_copy(m_gl["wglHi"][:, :], m_gla["kg"][:, 0:256]))
                tt(m_gl["wglLo"][:, :], m_gla["kg"][:, 0:256], m_gl["wglHi"][:, :].bitcast(F32), ALU.subtract).then_inc(S("wgl_ready"), 1)
                dve.wait_ge(S("wgl_ready"), 1)
                norm(6, "gla_norm_2")
                dve.wait_ge(S("gqk_free"), 4 + 8)

                def chunkless(ap):
                    return v3(ap, NGC)

                def gla_head(hd):
                    q, k = tile(m["gQK"], 2 * hd), tile(m["gQK"], 2 * hd + 1)
                    dve.wait_ge(S("lg_log"), hd + 1)
                    lg2 = m["lg"][:, :]
                    chain(stt3(lg2, lg2, 0.0, m["diff"][:, :], ALU.min, ALU.subtract))
                    for d in range(2):
                        lg, cum, diff = (tile(m[name], d) for name in ("lg", "kg", "diff"))
                        if d == 0:
                            chain(dve.tensor_tensor_scan(cum, m["m64"][:, :], lg, 0.0, ALU.mult, ALU.add))
                        else:
                            chain(dve.tensor_tensor_scan(cum[:, ::-1], m["m64"][:, :], lg[:, ::-1], 0.0, ALU.mult, ALU.add))
                        at = (GC - 1) * (1 - d)
                        last = chunkless(cum)[:, :, at:at + 1].broadcast_to([P, NGC, GC])
                        tt(chunkless(diff), last, chunkless(cum), ALU.subtract).then_inc(S("gcum"), 1)
                    for d in range(2):
                        for e, (name, by) in enumerate((("qg", q), ("kg", k), ("diff", k))):
                            dve.wait_ge(S("g_exp"), 6 * hd + 3 * d + e + 1)
                            tt(tile(m[name], d), by, tile(m[name], d), ALU.mult).then_inc(S("g_used"), 1)
                    dve.wait_ge(S("gdec_ready"), 2 * hd + 2)
                    for c in range(7):
                        dve.wait_ge(S("gu_mm"), 14 * hd + c + 1)
                        new = tile(m["gst"], c)
                        src = bank[4 + c % 2][:, :]
                        if c:
                            ins = stt3(new, tile(m["gst"], c - 1), m["gdec"][:, c:c + 1], src, ALU.mult, ALU.add)
                        else:
                            ins = dve.tensor_copy(new, src)
                        ins.then_inc(S("gs_ready"), 1)
                        dve.wait_ge(S("gs_ready"), 14 * hd + c + 1 + 1)
                    att = tile(m["lg"], 0)
                    for t in range(NT):
                        dve.wait_ge(S("gatt_mm"), 2 * hd + 2)
                        dve.sem_inc(S("gatt_seen"), 1)
                        dve.copy_predicated(m["attF"][:, :], m["mF"][:, :].bitcast(I32), bank[7][:, P * t:P * (t + 1)]).then_inc(S("attF_ready"), 1)
                        chain(dve.copy_predicated(m["attB"][:, :], m["mB"][:, :].bitcast(I32), bank[2][:, P * t:P * (t + 1)]))
                        dve.wait_ge(S("attF_ready"), 4 * hd + t + 1)
                        chain(tt(att[:, P * t:P * (t + 1)], m["attF"][:, :], m["attB"][:, :], ALU.add))
                    dve.sem_inc(S("att_ready"), 1)
                    for e in range(7):
                        c = 7 - e
                        dve.wait_ge(S("gu_mm"), 14 * hd + 7 + e + 1)
                        new, old = tile(m["gsb"], (c - 1) % 2), tile(m["gsb"], c % 2)
                        src = bank[4 + e % 2][:, :]
                        if e:
                            dve.wait_ge(S("go_mm"), 4 * hd + NT - (c + 1) // 2)
                        if e:
                            ins = stt3(new, old, m["gdec"][:, NGC + c:NGC + c + 1], src, ALU.mult, ALU.add)
                        else:
                            ins = dve.tensor_copy(new, src)
                        ins.then_inc(S("gs_ready"), 1)
                        dve.wait_ge(S("gs_ready"), 14 * hd + 7 + e + 1 + 1)

                with chain.loop(4, 3 + 8) as hd:
                    gla_head(hd)
                dve.wait_ge(S("go_free"), 16 + 1)
                ts(stat[:, 0:16], stat[:, 0:16], 1.0 / 512, EPS, ALU.mult, ALU.add).then_inc(S("gsq_mean"), 1)
                dve.wait_ge(S("gsq_root"), 1)
                chain(dve.reciprocal(stat[:, 0:16], stat[:, 0:16]))
                O = v3(m["gO"][:, :], NT)
                with dve.Fori(0, 4) as i:
                    for s in range(2):
                        for hf in range(2):
                            dve.wait_ge(S("gz_ready"), 4 * i + 2 * s + hf + 1 + 1)
                            for e in range(2):
                                o = O[:, 2 * hf + e, ds(512 * i + 256 * s, 256)]
                                ins = stt3(o, o, stat[:, ds(4 * (2 * hf + e) + i, 1)], m_gla2["gzs"][:, SEQ * hf + 256 * e:SEQ * hf + 256 * e + 256],
                                           ALU.mult, ALU.mult).then_inc(S("gate_half"), 1)
                            dve.wait_ge(S("gate_half"), 8 * i + 4 * s + 2 * hf + 2)
                            dve.sem_inc(S("gz_used"), 1)
                for k in range(IT):
                    turned_low("gy", lambda k: inner(k, m_gla2["gHi"], hHi), lambda k: inner(k, m_gla2["gLo"], hLo), "gla_onorm_2", 4, k)
                residual(R_GLA, 2, 2, lambda i, q: 2 * U_GLA_OUT + 4 * i + 2 * q + 2, 4, "gla_free")

            if on("end"):
                norm(7, "final_norm_2", 0, "x")
                dve.wait_ge(res_done, 8 * 9)

        @block.tensor
        def _(pe):
            def mark(ins):
                ins.then_inc(mm, 1)

            def product(dst, hi1, lo1, hi2, lo2, first, last):
                pe.matmul(dst, hi1, hi2, start=first, stop=False)
                pe.matmul(dst, hi1, lo2, start=False, stop=False)
                return pe.matmul(dst, lo1, hi2, start=False, stop=last)

            def chan(dst, s, at, Hi, Lo, ks, first=True, last=True, x0=0, normed=None):
                for n, k in enumerate(ks):
                    if normed is not None:
                        pe.wait_ge(h_ready, 8 * (normed - (normed > 4)) + k + 1)
                    w = slice(at(k), at(k) + P)
                    x = slice(SEQ * (k + x0), SEQ * (k + x0 + 1))
                    ins = product(dst, whi[s][:, w], wlo[s][:, w], Hi[:, x], Lo[:, x], first and n == 0, last and n == len(ks) - 1)
                return ins

            def tokens(s, hf, dst):
                for e in range(2):
                    for k in range(KT):
                        x = slice(SEQ * k + P * (2 * hf + e), SEQ * k + P * (2 * hf + e + 1))
                        w = slice(256 * k, 256 * k + 256)
                        ins = product(dst[:, 256 * e:256 * e + 256], hHi[:, x], hLo[:, x], whi[s][:, w], wlo[s][:, w], k == 0, k == KT - 1)
                return ins

            def unit(n):
                pe.wait_ge(w_lo, n + 1)

            def norm(j):
                for k in range(KT):
                    pe.wait_ge(S("sq_ready"), 8 * j + k + 1)
                    ins = pe.matmul(bank[4][:, :], ones[:, :], t32[k % 2][:, :], start=(k == 0), stop=(k == KT - 1))
                    ins.then_inc(S("sq_used"), 1)
                pe.wait_ge(S("sq_used"), 8 * j + 8)
                pe.sem_inc(S("sums"), 1)

            pair = lambda b: (lambda k: 256 * k + P * b)

            pe.wait_ge(S("cst"), 11)
            pe.wait_ge(S("vec_in"), 16 * (len(VEC_ROWS) + 3))
            vr = m_in["vrows"]
            pe.transpose(bank[4][:, 0:NVEC], vr[0:NVEC, 0:P], ident[0:NVEC, 0:NVEC]).then_inc(S("vec_turned"), 1)
            pe.transpose(bank[4][:, P:2 * P], vr[:, P:2 * P], ident[:, :]).then_inc(S("vec_turned"), 1)
            pe.transpose(bank[4][:, 2 * P:2 * P + 64], vr[0:64, 2 * P:3 * P], ident[0:64, 0:64]).then_inc(S("vec_turned"), 1)
            pe.wait_ge(S("x_in"), 16)
            for k in range(KT):
                if k >= 4:
                    pe.wait_ge(res_done, k - 3)
                for t in range(NT):
                    ins = pe.transpose(bank[k % 4][:, P * t:P * (t + 1)], m_in["xtok"][:, DM * t + P * k:DM * t + P * (k + 1)], ident[:, :])
                ins.then_inc(S("x_turn"), 1)
            pe.wait_ge(S("vec_ready"), 2)
            norm(0)

            with pe.Fori(0, 4) as i:
                for s in range(2):
                    unit(2 * i + s)
                    pe.wait_ge(S("cu_done" if s else "c_ready"), 2 * i + 1)
                    for b in range(2):
                        mark(chan(bank[2 * s + b][:, :], s, pair(b), hHi, hLo, range(KT), normed=None if s or b else 0))
            pe.wait_ge(S("cu_done"), 8 + 1)
            with pe.Fori(0, 2) as i:
                for s in range(2):
                    unit(U_CONV_B + 2 * i + s)
                    for b in range(2):
                        pe.wait_ge(S("y_free"), 4 * i + 2 * s + b + 1)
                        mark(chan(bank[2 * s + b][:, :], s, pair(b), hHi, hLo, range(KT)))

            def out8(u0, free, Hi, Lo):
                with pe.Fori(0, 2) as i:
                    for s in range(2):
                        unit(u0 + 2 * i + s)
                        for b in range(2):
                            pe.wait_ge(S(free), 4 * i + 2 * s + b + 1)
                            mark(chan(bank[2 * s + b][:, :], s, pair(b), Hi, Lo, range(KT)))

            def turn(name, src, k):
                if k >= 4:
                    pe.wait_ge(S(name + "_lo"), k - 3)
                for t in range(NT):
                    ins = pe.transpose(bank[k % 4][:, P * t:P * (t + 1)], src[:, DI * t + P * k:DI * t + P * (k + 1)], ident[:, :])
                ins.then_inc(S(name + "_turned"), 1)

            def out16(u0, free, Hi, Lo):
                with pe.Fori(0, 4) as i:
                    for s in range(2):
                        unit(u0 + 2 * i + s)
                        pe.wait_ge(S(free), 2 * i + s + 1)
                        mark(chan(bank[s][:, :], s, lambda k: P * k, hHi, hLo, range(8), True, False))
                        mark(chan(bank[s][:, :], s, lambda k: P * k, Hi, Lo, range(8, 16), False, True, x0=-8))

            pe.wait_ge(S("y_ready"), 1)
            out8(U_CONV_OUT, "conv_free", m_conv["yHi"], m_conv["yLo"])

            def ffn(j, u_up, u_down):
                norm(2 * j + 1)
                aHi, aLo = m_ffn[j][f"f{j}aHi"], m_ffn[j][f"f{j}aLo"]
                with pe.Fori(0, FT // 2) as i:
                    for s in range(2):
                        unit(u_up + 2 * i + s)
                        pe.wait_ge(S(f"a_done{j}" if s else f"sil_ready{j}"), 2 * i + 1)
                        for b in range(2):
                            mark(chan(bank[2 * s + b][:, :], s, pair(b), hHi, hLo, range(KT), normed=None if s or b else 2 * j + 1))
                pe.wait_ge(S(f"a_done{j}"), FT + 1)
                with pe.Fori(0, 4) as i:
                    for q in range(2):
                        pe.wait_ge(S(f"ffn_free{j}"), 2 * i + q + 1)
                        for s in range(2):
                            unit(u_down + 4 * i + 2 * q + s)
                            ks = range(HALF_FFN * s, HALF_FFN * (s + 1))
                            at = lambda k: P * (k - HALF_FFN * s)
                            mark(chan(bank[q][:, :], s, at, aHi, aLo, ks[:5], s == 0, False))
                            mark(chan(bank[q][:, :], s, at, aHi, aLo, ks[5:], False, s == 1))

            if on("ffn0"):
                ffn(0, U_FFN0, U_DOWN0)

            if on("attn"):
                pe.wait_ge(S("bias_in"), 32)
                pe.wait_ge(S("rb_one"), 1)
                pe.matmul(bank[5][0:HEADS, :], m_att["rb"][:, :], m_att["bkt"][:, 0:SEQ], start=True, stop=True).then_inc(S("toe_mm"), 1)
                pe.matmul(bank[6][0:HEADS, 0:P], m_att["rb"][:, :], m_att["bkt"][:, SEQ:640], start=True, stop=True).then_inc(S("toe_mm"), 1)
                norm(2)
                with pe.Fori(0, 4) as i:
                    for s in range(2):
                        unit(U_QKV + 2 * i + s)
                        for b in range(2):
                            pe.wait_ge(S("qkv_free"), 4 * i + 2 * s + b + 1)
                            mark(chan(bank[2 * s + b][:, :], s, pair(b), hHi, hLo, range(KT), normed=None if s or b else 2))
                with pe.Fori(0, 2) as i:
                    for s in range(2):
                        unit(U_QKV + 8 + 2 * i + s)
                        for hf in range(2):
                            pe.wait_ge(S("qkv_free"), 16 + 4 * i + 2 * s + hf + 1)
                            mark(tokens(s, hf, bank[2 * s + hf]))

                def scores(pr, hh):
                    hd = 2 * pr + hh
                    rows = slice(64 * hh, 64 * hh + 64)
                    pe.wait_ge(S("qs_ready"), 2 * pr + 2)
                    if hh or not isinstance(pr, int):
                        pe.wait_ge(S("scored"), 4 * hd)
                    for i in S_ORDER:
                        w = P * (i + 1)
                        dst = [bank[4][:, 0:128], bank[5][:, 0:256], bank[4][:, 128:512], bank[6][:, :]][i]
                        pe.matmul(dst, m_att["qS"][rows, P * i:P * (i + 1)], m_att["kS"][rows, 0:w], start=True, stop=True)\
                            .then_inc(S("scores"), 1)

                def turn_rows(pr, hh):
                    hd, prob = 2 * pr + hh, m_att[f"prob{hh}"]
                    pe.wait_ge(S("prob_ready"), 4 * hd + 4)
                    pe.wait_ge(S("pt_ready"), 4 * hd + 1)
                    for j in range(NT):
                        for i in range(j, NT):
                            at = 64 * i * (i + 1) + P * j
                            ins = pe.transpose(bank[j][:, P * (i - j):P * (i - j + 1)], prob[:, at:at + P], ident[:, :])
                        ins.then_inc(S("prob_turned"), 1)

                def weigh(pr, hh):
                    hd, pT = 2 * pr + hh, m_att["pT"]
                    pe.wait_ge(S("pt_ready"), 4 * hd + 4 + 1)
                    pe.wait_ge(S("o_done"), hd + 1)
                    for i in range(NT):
                        for j in range(i + 1):
                            at = [0, 512, 896, 1152][j] + P * (i - j)
                            ins = pe.matmul(bank[7][:, 64 * i:64 * i + 64], pT[:, at:at + P], m_att["vtok"][:, ds(DM * j + 64 * hd, 64)],
                                            start=(j == 0), stop=(j == i))
                    ins.then_inc(S("pv"), 1)

                pe.wait_ge(S("qkv_free"), 4 + 16 + 8)
                scores(0, 0)
                scores(0, 1)
                with pe.Fori(0, HEADS // 2 - 1) as pr:
                    for hh in range(2):
                        turn_rows(pr, hh)
                        scores(pr + 1, hh)
                        weigh(pr, hh)
                for hh in range(2):
                    turn_rows(HEADS // 2 - 1, hh)
                    weigh(HEADS // 2 - 1, hh)
                pe.wait_ge(S("o_done"), HEADS + 1)
                for k in range(KT):
                    if k >= 4:
                        pe.wait_ge(S("ho_ready"), k - 3)
                    for t in range(NT):
                        ins = pe.transpose(bank[k % 4][:, P * t:P * (t + 1)], m_att["otok"][:, DM * t + P * k:DM * t + P * (k + 1)], ident[:, :])
                    ins.then_inc(S("o_turned"), 1)
                pe.wait_ge(S("ho_ready"), 8)
                out8(U_ATTN_OUT, "att_free", hHi, hLo)

            if on("ffn1"):
                ffn(1, U_FFN1, U_DOWN1)
            if on("mid"):
                norm(4)

            if on("ssd"):
                m = m_ssd

                def project(g, q, normed=None):
                    if q % 2 == 0:
                        unit(U_XBC + 2 * g + q // 2)
                    mark(chan(bank[q][:, :], q // 2, pair(q % 2), hHi, hLo, range(KT), normed=normed))

                norm(5)
                project(0, 0, normed=5)
                pe.wait_ge(S("wdt_ready"), 1)
                for c in range(NT):
                    for k in range(KT):
                        x = slice(SEQ * k + P * c, SEQ * k + P * (c + 1))
                        w = slice(64 * k, 64 * k + 64)
                        ins = product(bank[4][:, 64 * c:64 * c + 64], hHi[:, x], hLo[:, x], m["wdtHi"][:, w], m["wdtLo"][:, w], k == 0, k == KT - 1)
                ins.then_inc(S("dt_mm"), 1)
                for q in range(1, 4):
                    project(0, q)
                pe.wait_ge(S("la_ready"), 1)
                for c in range(NT):
                    for d in range(2):
                        w = slice(64 * c + 32 * d, 64 * c + 32 * d + 32)
                        for b, mat in ((5, (LE, GE)[d]), (6, (GT, LT)[d]), (7, ones)):
                            ins = pe.matmul(bank[b][:, w], mat[:, :], m["la"][:, w], start=True, stop=True)
                ins.then_inc(S("decays"), 1)
                pe.wait_ge(S("decay_exp"), 3)
                pe.wait_ge(S("xpad_edge"), 2)

                def segments(g, c, d):
                    pe.wait_ge(S("rm_ready"), 8 * g + 2 * c + d + 1)
                    pe.matmul(bank[4 + d][:, :], (GT, LT)[d][:, :], m["Rm"][:, SEQ * d:SEQ * (d + 1)], start=True, stop=True).then_inc(S("seg"), 1)

                def group(g, more):
                    xc, bt = m["xc"], m["bt"]
                    BT, CT = tile(xc, 2), tile(xc, 3)
                    pe.wait_ge(S("xc_ready"), 4 * g + 2)
                    for b in range(2):
                        for e in range(2):
                            for q in range(2):
                                c = 2 * b + e
                                ins = pe.transpose(bank[4 + b][:, 256 * e + P * q:256 * e + P * (q + 1)], xc[:, SEQ * q + P * c:SEQ * q + P * (c + 1)], ident[:, :])
                        ins.then_inc(S("x_turned"), 1)
                    pe.wait_ge(S("xc_ready"), 4 * g + 4)
                    pe.wait_ge(S("y_bank_free"), 4 * g + 1)
                    for c in range(NT):
                        ins = pe.transpose(bank[6][:, P * c:P * (c + 1)], BT[:, P * c:P * (c + 1)], ident[:, :])
                    ins.then_inc(S("x_turned"), 1)
                    for c in range(NT):
                        ins = pe.matmul(bank[7][:, P * c:P * (c + 1)], BT[:, P * c:P * (c + 1)], CT[:, P * c:P * (c + 1)], start=True, stop=True)
                    ins.then_inc(S("cb_mm"), 1)
                    if more:
                        project(g + 1, 0)
                    pe.wait_ge(S("xt_ready"), 3 * g + 3)
                    for step in range(3):
                        if step:
                            pe.wait_ge(S("state_ready"), 3 * g + step)
                        for d in range(2):
                            c = ssd_chunk(step, d)
                            pe.wait_ge(S("xw_ready"), 6 * g + 2 * step + d + 1)
                            pe.matmul(bank[4 + d][:, 0:256], bt[:, P * c:P * (c + 1)], xw_buf(step, d), start=True, stop=True).then_inc(S("state_mm"), 1)
                    pe.wait_ge(S("state_ready"), 3 * g + 3)
                    for d in range(2):
                        segments(g, 0, d)
                    for c in range(NT):
                        if more and c < 3:
                            project(g + 1, c + 1)
                        pe.wait_ge(S("y_bank_free"), 4 * g + c + 1)
                        for d in range(2):
                            if not (c == 0 and d == 0) and not (c == 3 and d == 1):
                                ins = pe.matmul(bank[7][:, 256 * d:256 * d + 256], CT[:, P * c:P * (c + 1)], m["stt"][:, 1024 * d + 256 * c:1024 * d + 256 * c + 256],
                                                start=True, stop=True)
                        if c == 3:
                            ins.then_inc(S("c_read"), 1)
                        else:
                            for d in range(2):
                                pe.wait_ge(S("ex_ready"), 8 * g + 2 * c + d + 1)
                                segments(g, c + 1, d)
                        pe.wait_ge(S("xdt_ready"), 8 * g + 2 * c + 2)
                        pe.wait_ge(S("mt_ready"), 8 * g + 2 * c + 2)
                        for h in range(HPG):
                            for d in range(2):
                                at = 2 * (c % 2) + d
                                ins = pe.matmul(bank[6][:, 64 * h:64 * h + 64], m["MT"][:, SEQ * at + P * h:SEQ * at + P * (h + 1)],
                                                m["xdt"][:, 256 * at + 64 * h:256 * at + 64 * h + 64], start=(d == 0), stop=(d == 1))
                        ins.then_inc(S("y_mm"), 1)

                with pe.Fori(0, SSD_GROUPS - 1) as g:
                    group(g, True)
                group(SSD_GROUPS - 1, False)
                with pe.Fori(0, 4) as i:
                    for s in range(2):
                        unit(U_SZ + 2 * i + s)
                        pe.wait_ge(S("sz_ready"), 4 * i + 0 + 1)
                        for hf in range(2):
                            mark(tokens(s, hf, bank[2 * s + hf]))
                for k in range(IT):
                    pe.wait_ge(S("sy_scaled"), k // 2 + 1)
                    turn("sy", m_ssd["sY"], k)
                pe.wait_ge(S("sy_lo"), IT)
                out16(U_SSD_OUT, "ssd_free", m_ssd2["sHi"], m_ssd2["sLo"])

            if on("gla"):
                m = m_gla
                norm(6)
                with pe.Fori(0, 2) as i:
                    for s in range(2):
                        unit(U_GQK + 2 * i + s)
                        for b in range(2):
                            pe.wait_ge(S("gqk_free"), 4 * i + 2 * s + b + 1)
                            mark(chan(bank[2 * s + b][:, :], s, pair(b), hHi, hLo, range(KT), normed=None if s or b else 6))
                pe.wait_ge(S("wgl_ready"), 1)
                for t in range(NT):
                    for k in range(KT):
                        x = slice(SEQ * k + P * t, SEQ * k + P * (t + 1))
                        w = slice(32 * k, 32 * k + 32)
                        ins = product(bank[4][:, 32 * t:32 * t + 32], hHi[:, x], hLo[:, x], m_gl["wglHi"][:, w], m_gl["wglLo"][:, w], k == 0, k == KT - 1)
                ins.then_inc(S("gl_mm"), 1)
                pe.wait_ge(S("gl_ready"), 1)
                for t in range(NT):
                    ins = pe.transpose(bank[5][0:32, P * t:P * (t + 1)], m_gl["gl"][:, 32 * t:32 * t + 32], ident[:, :])
                ins.then_inc(S("gl_turned"), 1)
                pe.wait_ge(S("gqk_free"), 4 + 8)
                pe.wait_ge(S("glT_ready"), 1)
                gv = m["gv"]
                with pe.Fori(0, 4) as hd:
                    def values(s, hf):
                        if hf == 0:
                            unit(U_GV + 2 * hd + s)
                        if s:
                            pe.wait_ge(S("gv_ready"), 4 * hd + hf + 1)
                        mark(tokens(s, hf, bank[hf]))

                    def increment(n):
                        d, c = (0, n) if n < 7 else (1, 14 - n)
                        r, t = c % 2, c // 2
                        if n >= 2:
                            pe.wait_ge(S("gs_ready"), 14 * hd + n - (2 if n % 7 > 1 else 1) + 1 + 1)
                        pe.matmul(bank[4 + (n % 7) % 2][:, :], t32[d][GC * r:GC * (r + 1), P * t:P * (t + 1)],
                                  gv[GC * r:GC * (r + 1), SEQ * t:SEQ * (t + 1)], start=True, stop=True).then_inc(S("gu_mm"), 1)

                    def keys(d):
                        pe.wait_ge(S("g_used"), 6 * hd + 3 * d + 3)
                        if d:
                            pe.wait_ge(S("kdt_ready"), 2 * hd + 1)
                        for t in range(NT):
                            ins = pe.transpose(bank[6][:, P * t:P * (t + 1)], m["diff"][:, SEQ * d + P * t:SEQ * d + P * (t + 1)], ident[:, :])
                        ins.then_inc(S("kd_turned"), 1)
                        for t in range(NT):
                            x = slice(SEQ * d + P * t, SEQ * d + P * (t + 1))
                            ins = pe.matmul(bank[2 if d else 7][:, P * t:P * (t + 1)], m["kg"][:, x], m["qg"][:, x], start=True, stop=True)
                        ins.then_inc(S("gatt_mm"), 1)

                    pe.wait_ge(S("gs_ready"), 14 * hd + 1)
                    for d in range(2):
                        pe.wait_ge(S("wgs_ready"), 2 * hd + d + 1)
                        pe.matmul(bank[4 + d][:, :], m["wgs"][:, P * d:P * (d + 1)], rstd[0:32, :], start=True, stop=True).then_inc(S("gate_mm"), 1)
                    pe.wait_ge(S("go_free"), 4 * hd + 1)
                    values(0, 0)
                    values(0, 1)
                    keys(0)
                    values(1, 0)
                    values(1, 1)
                    pe.wait_ge(S("gv_ready"), 4 * hd + 4)
                    pe.wait_ge(S("kdt_ready"), 2 * hd + 1)
                    increment(0)
                    increment(1)
                    keys(1)
                    for n in range(2, 7):
                        increment(n)
                    pe.wait_ge(S("kdt_ready"), 2 * hd + 2)
                    increment(7)
                    pe.wait_ge(S("att_ready"), hd + 1)
                    for n in range(NT):
                        t = NT - 1 - n
                        out = bank[0 if n % 2 else 3]
                        if n >= 2:
                            pe.wait_ge(S("go_free"), 4 * hd + n - 1 + 1)

                        def term(d, state, r, last):
                            c = 2 * t + r
                            return pe.matmul(out[GC * r:GC * (r + 1), :], m["qg"][:, SEQ * d + GC * c:SEQ * d + GC * (c + 1)], state,
                                             start=False, stop=last, skip_group_check=True)

                        pe.matmul(out[:, :], tile(m["lg"], 0)[:, P * t:P * (t + 1)], gv[:, SEQ * t:SEQ * (t + 1)], start=True, stop=False, skip_group_check=True)
                        for r in range(2):
                            if 2 * t + r:
                                term(0, tile(m["gst"], 2 * t + r - 1), r, 2 * t + r == 7)
                        pe.wait_ge(S("gs_ready"), 14 * hd + 8 + 2 * n + 1)
                        for e in range(2):
                            if t:
                                increment(8 + 2 * n + e)
                        for r in range(2):
                            if 2 * t + r < 7:
                                ins = term(1, tile(m["gsb"], r), r, True)
                        ins.then_inc(S("go_mm"), 1)
                with pe.Fori(0, 4) as i:
                    for s in range(2):
                        unit(U_GZ + 2 * i + s)
                        pe.wait_ge(S("gz_ready"), 4 * i + 1)
                        pe.wait_ge(S("go_free"), 16 + 1)
                        for hf in range(2):
                            mark(tokens(s, hf, bank[2 * s + hf]))
                pe.wait_ge(S("gz_used"), 16 + 1)
                for k in range(IT):
                    turn("gy", m_gla["gO"], k)
                pe.wait_ge(S("gy_lo"), IT)
                out16(U_GLA_OUT, "gla_free", m_gla2["gHi"], m_gla2["gLo"])

            if on("end"):
                norm(7)
            final = 8 * ((last_r + 1) if stages[-1] != "end" else 9)
            pe.wait_ge(res_done, final)
            for t in range(NT):
                for k in range(KT):
                    if KT * t + k >= 4:
                        pe.wait_ge(S("out_ready"), KT * t + k - 3)
                    pe.transpose(bank[k % 4][:, 0:P], xT[:, SEQ * k + P * t:SEQ * k + P * (t + 1)], ident[:, :]).then_inc(S("out_turned"), 1)


def kernel(**inputs):
    import numpy as _np
    import concourse.bacc as _bacc
    from concourse import mybir as _mybir
    from concourse.bass_utils import run_bass_kernel_spmd as _run

    nc = _bacc.Bacc("TRN2", target_bir_lowering=False, num_devices=1)
    arrays, aps = {}, {}
    given = {n: _np.ascontiguousarray(inputs[n]) for n in INPUTS}
    given["bucket_rows"] = bucket_rows()
    for name, a in given.items():
        arrays[f"in_{name}"] = a
        aps[name] = nc.dram_tensor(f"in_{name}", a.shape, _mybir.dt.from_np(a.dtype), kind="ExternalInput").ap()
    out = nc.dram_tensor("out_x", (1, SEQ, DM), F32, kind="ExternalOutput").ap()
    build(nc, aps, out)
    r = _run(nc, [arrays], core_ids=[0])
    return r.results[0]["out_x"]
```
